# Optimizing a Trainium2 kernel written in Bass

```python
import math
import jax, jax.numpy as jnp
from jax import lax
import numpy as np

D_MODEL = 1024
BATCH = 1
SEQ = 2048
DEPTH = 1

CHUNK = 64
HEAD_DIM = 64
A_HEADS = 8
A_WIDTH = A_HEADS * HEAD_DIM
LEFT_CHUNKS = 8
BAND = (LEFT_CHUNKS + 1) * CHUNK
MAX_REL = 128
B_HEADS = 4
B_QK_DIM = HEAD_DIM
B_V_DIM = 2 * HEAD_DIM
B_WIDTH = B_HEADS * B_V_DIM
MIX_WIDTH = A_WIDTH + B_WIDTH
IN_WIDTH = 3 * A_WIDTH + 2 * (B_HEADS * 2 * B_QK_DIM) + B_WIDTH
ROPE_THETA = 500000.0
ROPE_DIM = B_QK_DIM // 4
Q_BLOCK = 128
N_EXPERTS = 32
TOP_K = 4
D_EXPERT = D_MODEL
SWIGLU_LIMIT = 7.0
SWIGLU_ALPHA = 1.702
EPS = 1e-6
NEG_INF = -1e30
N_MOD = 6

kernel_name = "hybrid_chunked_diffattn_moe_block"

def rms_norm(x, g):
    xf = x.astype(jnp.float32)
    y = xf * lax.rsqrt(jnp.mean(xf * xf, axis=-1, keepdims=True) + EPS)
    return (y * g.astype(jnp.float32)).astype(x.dtype)

def modulate(h, shift, scale):
    return h * (1.0 + scale[:, None, :]) + shift[:, None, :]

def lambda_init_fn(layer_idx):
    return 0.8 - 0.6 * math.exp(-0.3 * layer_idx)

def partial_rope(x, cos, sin):
    half = ROPE_DIM // 2
    x1 = x[..., :half].astype(jnp.float32)
    x2 = x[..., half:ROPE_DIM].astype(jnp.float32)
    r1 = x1 * cos - x2 * sin
    r2 = x2 * cos + x1 * sin
    return jnp.concatenate([r1.astype(x.dtype), r2.astype(x.dtype), x[..., ROPE_DIM:]], axis=-1)

def chunked_relbias_attention(q, k, v, rel_table):
    b, s, h, d = q.shape
    nc = s // CHUNK
    qc = q.reshape(b, nc, CHUNK, h, d)
    pad = ((0, 0), (LEFT_CHUNKS * CHUNK, 0), (0, 0), (0, 0))
    kp = jnp.pad(k, pad).reshape(b, nc + LEFT_CHUNKS, CHUNK, h, d)
    vp = jnp.pad(v, pad).reshape(b, nc + LEFT_CHUNKS, CHUNK, h, d)
    kb = jnp.concatenate([kp[:, j:j + nc] for j in range(LEFT_CHUNKS + 1)], axis=2)
    vb = jnp.concatenate([vp[:, j:j + nc] for j in range(LEFT_CHUNKS + 1)], axis=2)
    rel = LEFT_CHUNKS * CHUNK + np.arange(CHUNK)[:, None] - np.arange(BAND)[None, :]
    rel_idx = np.clip(rel, -MAX_REL, MAX_REL) + MAX_REL
    bias = rel_table.astype(jnp.float32)[:, rel_idx]
    key_abs = (jnp.arange(nc)[:, None] - LEFT_CHUNKS) * CHUNK + jnp.arange(BAND)[None, :]
    valid = key_abs >= 0
    scores = jnp.einsum('bcihd,bcjhd->bhcij', qc, kb).astype(jnp.float32) * (d ** -0.5)
    scores = scores + bias[None, :, None, :, :]
    scores = jnp.where(valid[None, None, :, None, :], scores, NEG_INF)
    p = jax.nn.softmax(scores, axis=-1).astype(v.dtype)
    out = jnp.einsum('bhcij,bcjhd->bcihd', p, vb)
    return out.reshape(b, s, h * d)

def differential_attention(q, k, v, lam, g_subln, lambda_init):
    b, s, h = q.shape[:3]
    nb = s // Q_BLOCK
    scale = B_QK_DIM ** -0.5
    key_chunk = jnp.arange(s) // CHUNK
    qb = q.reshape(b, nb, Q_BLOCK, h, 2, B_QK_DIM).transpose(1, 0, 2, 3, 4, 5)

    def block(args):
        q_blk, blk = args
        sc = jnp.einsum('bqhcd,bkhcd->bhcqk', q_blk, k).astype(jnp.float32) * scale
        q_chunk = (blk * Q_BLOCK + jnp.arange(Q_BLOCK)) // CHUNK
        mask = key_chunk[None, :] <= q_chunk[:, None]
        sc = jnp.where(mask[None, None, None], sc, NEG_INF)
        p = jax.nn.softmax(sc, axis=-1)
        w = (p[:, :, 0] - lam * p[:, :, 1]).astype(v.dtype)
        o = jnp.einsum('bhqk,bkhd->bqhd', w, v)
        return rms_norm(o, g_subln) * (1.0 - lambda_init)

    out = lax.map(block, (qb, jnp.arange(nb)))
    return out.transpose(1, 0, 2, 3, 4).reshape(b, s, h * B_V_DIM)

def moe_ffn(h, w_router, b_router, w_gate_up, b_gate_up, w_down, b_down):
    b, s, d = h.shape
    hf = h.reshape(-1, d)
    n_tok = hf.shape[0]
    logits = (hf @ w_router).astype(jnp.float32) + b_router.astype(jnp.float32)
    top_v, top_i = lax.top_k(logits, TOP_K)
    top_w = jax.nn.softmax(top_v, axis=-1)
    flat_e = top_i.reshape(-1)
    flat_w = top_w.reshape(-1)
    order = jnp.argsort(flat_e, stable=True)
    sorted_e = flat_e[order]
    tok = order // TOP_K
    xs = hf[tok]
    group_sizes = jnp.bincount(flat_e, length=N_EXPERTS).astype(jnp.int32)
    gu = lax.ragged_dot(xs, w_gate_up, group_sizes) + b_gate_up[sorted_e]
    gate = jnp.minimum(gu[:, :D_EXPERT], SWIGLU_LIMIT)
    up = jnp.clip(gu[:, D_EXPERT:], -SWIGLU_LIMIT, SWIGLU_LIMIT)
    act = (up + 1.0) * (gate * jax.nn.sigmoid(SWIGLU_ALPHA * gate))
    y = lax.ragged_dot(act, w_down, group_sizes) + b_down[sorted_e]
    y = y * flat_w[order][:, None].astype(y.dtype)
    return jax.ops.segment_sum(y, tok, num_segments=n_tok).reshape(b, s, d)

def setup_inputs(seed: int = 0) -> dict:
    key = jax.random.key(seed)
    ks = jax.random.split(key, 24)
    f32 = jnp.float32
    nrm = lambda k, shp, sc: jax.random.normal(k, shp, f32) * sc
    x = nrm(ks[0], (BATCH, SEQ, D_MODEL), 1.0)
    c = nrm(ks[1], (BATCH, D_MODEL), 1.0)
    offset = jax.random.randint(ks[2], (BATCH, 1), 0, SEQ, dtype=jnp.int32)
    positions = (jnp.arange(SEQ, dtype=jnp.int32)[None, :] + offset).astype(jnp.int32)
    return {
        "x": x,
        "c": c,
        "positions": positions,
        "w_ada": nrm(ks[3], (DEPTH, D_MODEL, N_MOD * D_MODEL), 0.5 * D_MODEL ** -0.5),
        "b_ada": nrm(ks[4], (DEPTH, N_MOD * D_MODEL), 0.02),
        "g_mix_norm": 1.0 + nrm(ks[5], (DEPTH, D_MODEL), 0.02),
        "w_in": nrm(ks[6], (DEPTH, D_MODEL, IN_WIDTH), D_MODEL ** -0.5),
        "rel_bias": nrm(ks[7], (DEPTH, A_HEADS, 2 * MAX_REL + 1), 0.5),
        "lambda_q1": nrm(ks[8], (DEPTH, B_QK_DIM), 0.1),
        "lambda_k1": nrm(ks[9], (DEPTH, B_QK_DIM), 0.1),
        "lambda_q2": nrm(ks[10], (DEPTH, B_QK_DIM), 0.1),
        "lambda_k2": nrm(ks[11], (DEPTH, B_QK_DIM), 0.1),
        "g_subln": 1.0 + nrm(ks[12], (DEPTH, B_V_DIM), 0.02),
        "w_out": nrm(ks[13], (DEPTH, MIX_WIDTH, D_MODEL), MIX_WIDTH ** -0.5),
        "g_ffn_norm": 1.0 + nrm(ks[14], (DEPTH, D_MODEL), 0.02),
        "w_router": nrm(ks[15], (DEPTH, D_MODEL, N_EXPERTS), D_MODEL ** -0.5),
        "b_router": nrm(ks[16], (DEPTH, N_EXPERTS), 0.01),
        "w_gate_up": nrm(ks[17], (DEPTH, N_EXPERTS, D_MODEL, 2 * D_EXPERT), D_MODEL ** -0.5),
        "b_gate_up": nrm(ks[18], (DEPTH, N_EXPERTS, 2 * D_EXPERT), 0.02),
        "w_down": nrm(ks[19], (DEPTH, N_EXPERTS, D_EXPERT, D_MODEL), D_EXPERT ** -0.5),
        "b_down": nrm(ks[20], (DEPTH, N_EXPERTS, D_MODEL), 0.02),
        "g_final": 1.0 + nrm(ks[21], (D_MODEL,), 0.02),
    }

def reference(x, c, positions, w_ada, b_ada, g_mix_norm, w_in, rel_bias, lambda_q1, lambda_k1,
              lambda_q2, lambda_k2, g_subln, w_out, g_ffn_norm, w_router, b_router, w_gate_up,
              b_gate_up, w_down, b_down, g_final):
    b, s, _ = x.shape
    inv_freq = ROPE_THETA ** (-jnp.arange(0, ROPE_DIM, 2, dtype=jnp.float32) / ROPE_DIM)
    ang = positions.astype(jnp.float32)[..., None] * inv_freq
    cos = jnp.cos(ang)[:, :, None, None, :]
    sin = jnp.sin(ang)[:, :, None, None, :]
    c_act = jax.nn.silu(c)
    qk_b = B_HEADS * 2 * B_QK_DIM
    for l in range(DEPTH):
        mod = c_act @ w_ada[l] + b_ada[l]
        sh_m, sc_m, gt_m, sh_f, sc_f, gt_f = jnp.split(mod, N_MOD, axis=-1)
        lambda_init = lambda_init_fn(l)

        h = modulate(rms_norm(x, g_mix_norm[l]), sh_m, sc_m)
        proj = h @ w_in[l]
        q_a, k_a, v_a, q_b, k_b, v_b = jnp.split(
            proj, np.cumsum([A_WIDTH, A_WIDTH, A_WIDTH, qk_b, qk_b]).tolist(), axis=-1)
        shp_a = (b, s, A_HEADS, HEAD_DIM)
        o_a = chunked_relbias_attention(q_a.reshape(shp_a), k_a.reshape(shp_a),
                                        v_a.reshape(shp_a), rel_bias[l])
        shp_b = (b, s, B_HEADS, 2, B_QK_DIM)
        q_b = partial_rope(q_b.reshape(shp_b), cos, sin)
        k_b = partial_rope(k_b.reshape(shp_b), cos, sin)
        lam = (jnp.exp(jnp.sum(lambda_q1[l].astype(jnp.float32) * lambda_k1[l].astype(jnp.float32)))
               - jnp.exp(jnp.sum(lambda_q2[l].astype(jnp.float32) * lambda_k2[l].astype(jnp.float32)))
               + lambda_init)
        o_b = differential_attention(q_b, k_b, v_b.reshape(b, s, B_HEADS, B_V_DIM), lam,
                                     g_subln[l], lambda_init)
        mix = jnp.concatenate([o_a, o_b], axis=-1) @ w_out[l]
        x = x + gt_m[:, None, :] * mix

        h = modulate(rms_norm(x, g_ffn_norm[l]), sh_f, sc_f)
        ffn = moe_ffn(h, w_router[l], b_router[l], w_gate_up[l], b_gate_up[l], w_down[l], b_down[l])
        x = x + gt_f[:, None, :] * ffn
    return rms_norm(x, g_final)


_drawn_inputs = setup_inputs


def setup_inputs(seed=0):
    import zlib

    import numpy as np

    out = dict(_drawn_inputs(seed))
    spreads = {}
    factors = {'g_mix_norm': 8.0,
     'rel_bias': 3.832,
     'lambda_q1': 4.527,
     'lambda_k1': 8.0,
     'lambda_q2': 200.0,
     'g_subln': 21.577,
     'g_ffn_norm': 3.436,
     'b_router': 4.693,
     'b_gate_up': 8.0,
     'b_down': 39.611,
     'g_final': 20.142,
     'lambda_k2': 3.482}
    for name, (base, spread) in spreads.items():
        noise = np.random.default_rng([zlib.crc32(name.encode()), seed]).standard_normal(out[name].shape)
        drawn = base * np.exp(spread * noise) if base else spread * noise
        out[name] = __import__('jax').numpy.asarray(drawn.astype(out[name].dtype))
    for name, factor in factors.items():
        out[name] = (out[name] * factor).astype(out[name].dtype)
    return out
```

```python
from contextlib import ExitStack

import numpy as np

import concourse.bass as bass
from concourse import mybir

P = 128
D = 1024
KT = D // P
SEQ = 2048
NT = SEQ // P
NG4 = SEQ // 512
NMOD = 6
HD = 64
A_HEADS = 8
B_HEADS = 4
AW = A_HEADS * HD
BW = B_HEADS * 2 * HD
IN_W = 3 * AW + 2 * BW + BW
UNITS = 4
BAND_T = 5
BAND = BAND_T * P
MAX_REL = 128
RELW = 2 * MAX_REL + 1
TOE = BAND + P - 1
NE = 32
TOPK = 4
CAP = SEQ
ROWS = SEQ + P
ALPHA = 1.702
LIMIT = 7.0
EPS = 1e-6
NEG = -1e30
LAM0 = 0.8 - 0.6
ROPE_HALF = 8
SCALE = HD ** -0.5

F32 = mybir.dt.float32
F32R = mybir.dt.float32r
I32 = mybir.dt.int32
U32 = mybir.dt.uint32
ALU = mybir.AluOpType
ACT = mybir.ActivationFunctionType
AX = mybir.AxisListType.X


class Chain:

    def __init__(self, eng, sem, base=0):
        self.eng, self.sem, self.base, self.n = eng, sem, base, 0

    def add(self, ins):
        ins.then_inc(self.sem, 1)
        self.n += 1
        return self.base + self.n

    def link(self, ins):
        self.add(ins)
        self.eng.wait_ge(self.sem, self.base + self.n)


def hold(eng, started, *waits):
    values = [(s, v if isinstance(v, int) else eng.to_reg(v)) for s, v in waits]
    eng.wait_ge(started, 1)
    for s, v in values:
        eng.wait_ge(s, v)


def build_program(nc, io):
    with ExitStack() as top:
        persistent = top

        def sb(ctx, name, shape, dt=F32):
            return ctx.enter_context(nc.sbuf_tensor(name, shape, dt))

        taken = []

        def sem(name):
            taken.append(nc.alloc_semaphore(name=name))
            return taken[-1]

        bank = [top.enter_context(nc.psum_tensor(f"bank{i}", [P, 512], F32)) for i in range(8)]
        ident = sb(persistent, "ident", [P, P])
        loaded = sem("constants_loaded")
        mod_d, o_d, acc_d, h2_d, list_d, toe_d = (
            io["mod_scratch"], io["o_scratch"], io["acc_scratch"], io["h2_scratch"],
            io["list_scratch"], io["toe_scratch"])

        stage1_and_2(nc, io, top, sb, sem, bank, ident, loaded, mod_d, o_d, toe_d)
        nc.clear_and_free_semaphores(taken)
        nc.all_engine_barrier()
        table = sb(persistent, "tile_table", [1, 128], I32)
        stage3(nc, io, sb, sem, bank, ident, mod_d, o_d, acc_d, h2_d, list_d, table)
        stage4(nc, io, sb, sem, bank, ident, mod_d, acc_d, h2_d, list_d, table)
        stage5(nc, io, sb, sem, acc_d)


def stage1_and_2(nc, io, top, sb, sem, bank, ident, loaded, mod_d, o_d, toe_d):
    with ExitStack() as ctx:
        hT = sb(ctx, "hT", [P, KT, SEQ])
        cosT = sb(ctx, "cosT", [P, SEQ])
        sinT = sb(ctx, "sinT", [P, SEQ])
        rot = sb(ctx, "rot", [P, P])
        stage1(nc, io, sb, sem, bank, ident, loaded, mod_d, toe_d, hT, cosT, sinT, rot)
        stage2(nc, io, sb, sem, bank, ident, o_d, toe_d, hT, cosT, sinT, rot)


def stage1(nc, io, sb, sem, bank, ident, loaded, mod_d, toe_d, hT, cosT, sinT, rot):
    NCH = NMOD * D // 512
    with ExitStack() as ctx:
        ccol = sb(ctx, "ccol", [P, KT])
        csig = sb(ctx, "csig", [P, KT])
        cact = sb(ctx, "cact", [P, KT])
        gmix = sb(ctx, "gmix", [P, KT])
        one = sb(ctx, "one", [1, 1])
        wada = sb(ctx, "wada", [P, 2, KT, 512])
        bada = sb(ctx, "bada", [1, 2, 512])
        mrow = sb(ctx, "mrow", [1, 2, 512])
        mcol = sb(ctx, "mcol", [P, 2 * KT])
        gcol = sb(ctx, "gcol", [P, KT])
        xt = sb(ctx, "xt", [P, 4, D])
        xsq = sb(ctx, "xsq", [P, D])
        xss = sb(ctx, "xss", [P, 4])
        xrs = sb(ctx, "xrs", [P, 4])
        xms = sb(ctx, "xms", [P, 4])
        xrt = sb(ctx, "xrt", [P, 4])
        posi = sb(ctx, "posi", [P, SEQ], I32)
        ang = sb(ctx, "ang", [P, SEQ])
        kk = sb(ctx, "kk", [P, SEQ])
        kh = sb(ctx, "kh", [P, SEQ])
        freq = sb(ctx, "freq", [P, 1])
        relr = sb(ctx, "relr", [A_HEADS, RELW])
        toe = sb(ctx, "toe", [A_HEADS, TOE])

        w_in = [sem(f"ada_loaded{i}") for i in range(2)]
        b_in = [sem(f"ada_bias_loaded{i}") for i in range(2)]
        m_mm = sem("mod_product")
        m_add = sem("mod_added")
        m_out = [sem(f"mod_stored{i}") for i in range(2)]
        c_rdy = sem("c_activated")
        csg = sem("c_sigmoid")
        mc_mm = sem("mod_columns_product")
        mc_ok = sem("mod_columns_ready")
        x_in = sem("x_loaded")
        ss_ok = sem("x_squares_summed")
        xn_ok = sem("x_normalised")
        ms_ok = sem("x_mean_square")
        rt_ok = sem("x_root")
        xt_mm = sem("x_transposed")
        h_ok = sem("h_columns_written")
        vch = sem("stage1_vector_chain")
        angs = sem("angles_reduced")
        abss = sem("cos_argument_ready")
        trig = sem("tables_written")
        toes = sem("toeplitz_built")
        pch = sem("stage1_pool_chain")
        toe_out = sem("toeplitz_stored")
        bias_out = sem("bias_tiles_stored")

        with nc.Block() as block:
            @block.sync
            def _(sp):
                sp.dma_start(ccol[:, :], io["c_col"]).then_inc(loaded, 16)
                sp.dma_start(gmix[:, :], io["g_mix_col"]).then_inc(loaded, 16)
                sp.dma_start(ident[:, :], io["ident"]).then_inc(loaded, 16)
                sp.dma_start(rot[:, :], io["rot"]).then_inc(loaded, 16)
                sp.dma_start(freq[:, :], io["freq"]).then_inc(loaded, 16)
                sp.dma_start(posi[:, :], io["positions"].broadcast_to([P, SEQ])).then_inc(loaded, 16)
                sp.dma_start(relr[:, :], io["rel_rev"]).then_inc(loaded, 16)
                for n in range(NCH):
                    if n >= 2:
                        sp.wait_ge(m_mm, n - 1)
                    sp.dma_start(wada[:, n % 2], io["w_ada"][:, n * 512:(n + 1) * 512]
                                 .rearrange("(k p) n -> p k n", p=P)).then_inc(w_in[n % 2], 16)
                    if n >= 2:
                        sp.wait_ge(m_add, n - 1)
                    sp.dma_start(bada[:, n % 2, :], io["b_ada"][:, n * 512:(n + 1) * 512]).then_inc(b_in[n % 2], 16)
                sp.wait_ge(toe_out, 16)
                for h in range(A_HEADS):
                    sp.dma_start(io["bias_scratch"][h], toe_d[h:h + 1, :].broadcast_to([P, TOE])).then_inc(bias_out, 16)
                sp.wait_ge(bias_out, 16 * A_HEADS)

            @block.tensor
            def _(pe):
                pe.wait_ge(c_rdy, 1)
                for n in range(NCH):
                    pe.wait_ge(w_in[n % 2], 16 * (n // 2 + 1))
                    if n >= 2:
                        pe.wait_ge(m_add, n - 1)
                    for k in range(KT):
                        mm = pe.matmul(bank[n % 2][0:1, :], cact[:, k:k + 1], wada[:, n % 2, k, :],
                                       start=(k == 0), stop=(k == KT - 1))
                    mm.then_inc(m_mm, 1)
                    if n < 4:
                        pe.wait_ge(m_add, n + 1)
                        for j in range(4):
                            mm = pe.matmul(bank[2][:, 4 * n + j:4 * n + j + 1],
                                           mrow[0:1, n % 2, j * P:(j + 1) * P], one[0:1, 0:1],
                                           start=True, stop=True)
                        mm.then_inc(mc_mm, 1)
                for g in range(NG4):
                    pe.wait_ge(xn_ok, 4 * (g + 1))
                    for k in range(KT):
                        n = g * KT + k
                        if n >= 4:
                            pe.wait_ge(h_ok, n - 3)
                        for j in range(4):
                            mm = pe.transpose(bank[4 + n % 4][:, j * P:(j + 1) * P],
                                              xt[:, j, k * P:(k + 1) * P], ident[:, :])
                        mm.then_inc(xt_mm, 1)

            @block.scalar
            def _(act):
                act.wait_ge(loaded, 16 * 7)
                act.activation(csig[:, :], ccol[:, :], ACT.Sigmoid).then_inc(csg, 1)
                for g in range(NG4):
                    if g >= 1:
                        act.wait_ge(xt_mm, KT * g)
                    for j in range(4):
                        t = 4 * g + j
                        act.dma_start(xt[:, j, :], io["x"][t * P:(t + 1) * P, :]).then_inc(x_in, 16)
                    act.wait_ge(x_in, 64 * (g + 1))
                    for j in range(4):
                        t = 4 * g + j
                        if t >= 1:
                            act.wait_ge(ss_ok, t)
                        act.activation(xsq[:, :], xt[:, j, :], ACT.Square,
                                       accum_out=xss[:, j:j + 1]).then_inc(ss_ok, 1)
                    act.wait_ge(ms_ok, g + 1)
                    act.activation(xrt[:, :], xms[:, :], ACT.Sqrt).then_inc(rt_ok, 1)
                    if g == 0:
                        act.wait_ge(angs, 1)
                        act.activation(sinT[:, :], ang[:, :], ACT.Sin).then_inc(trig, 1)
                        act.wait_ge(abss, 1)
                        act.activation(cosT[:, :], kk[:, :], ACT.Sin).then_inc(trig, 1)

            @block.vector
            def _(dve):
                ch = Chain(dve, vch)
                ch.link(dve.memset(one[:, :], 1.0))
                dve.wait_ge(loaded, 16 * 7)
                dve.wait_ge(csg, 1)
                dve.tensor_tensor(cact[:, :], ccol[:, :], csig[:, :], ALU.mult).then_inc(c_rdy, 1)
                two_pi = 2.0 * np.pi
                parts, rest = [], two_pi
                for bits in (2 ** 9, 2 ** 21, 2 ** 33):
                    part = float(np.floor(rest * bits) / bits)
                    parts.append(part)
                    rest -= part
                parts.append(rest)
                magic = 1.5 * 2.0 ** 23
                big = magic * 4096.0
                ch.link(dve.tensor_copy(ang[:, :], posi[:, :]))
                ch.link(dve.tensor_scalar(ang[:, :], ang[:, :], freq[:, 0:1], None, ALU.mult))
                ch.link(dve.tensor_scalar(kk[:, :], ang[:, :], 1.0 / two_pi, None, ALU.mult))
                ch.link(dve.tensor_scalar(kk[:, :], kk[:, :], magic, None, ALU.add))
                ch.link(dve.tensor_scalar(kk[:, :], kk[:, :], -magic, None, ALU.add))
                ch.link(dve.tensor_scalar(kh[:, :], kk[:, :], big, None, ALU.add))
                ch.link(dve.tensor_scalar(kh[:, :], kh[:, :], -big, None, ALU.add))
                ch.link(dve.tensor_tensor(kk[:, :], kk[:, :], kh[:, :], ALU.subtract))
                for part in parts:
                    for m in (kh, kk):
                        ch.link(dve.scalar_tensor_tensor(ang[:, :], m[:, :], -part, ang[:, :],
                                                         ALU.mult, ALU.add))
                ch.link(dve.tensor_scalar(ang[:, :], ang[:, :], float(np.float32(3.1415925)),
                                          float(np.float32(-3.1415925)), ALU.min, ALU.max))
                dve.sem_inc(angs, 1)
                ch.link(dve.scalar_tensor_tensor(kk[:, :], ang[:, :], -1.0, ang[:, :], ALU.mult, ALU.max))
                dve.tensor_scalar(kk[:, :], kk[:, :], -1.0, float(np.pi / 2), ALU.mult, ALU.add).then_inc(abss, 1)
                for n in range(NCH):
                    dve.wait_ge(m_mm, n + 1)
                    dve.wait_ge(b_in[n % 2], 16 * (n // 2 + 1))
                    if n >= 2:
                        dve.wait_ge(m_out[n % 2], 16 * (n // 2))
                        dve.wait_ge(mc_mm, min(n - 1, 4))
                    dve.tensor_tensor(mrow[:, n % 2, :], bank[n % 2][0:1, :], bada[:, n % 2, :],
                                      ALU.add).then_inc(m_add, 1)
                    if n == 3:
                        dve.wait_ge(mc_mm, 4)
                        ch.link(dve.tensor_copy(mcol[:, :], bank[2][:, 0:2 * KT]))
                        ch.link(dve.tensor_scalar(gcol[:, :], mcol[:, KT:2 * KT], 1.0, None, ALU.add))
                        ch.link(dve.tensor_tensor(gcol[:, :], gcol[:, :], gmix[:, :], ALU.mult))
                for g in range(NG4):
                    dve.wait_ge(ss_ok, 4 * (g + 1))
                    dve.tensor_scalar(xms[:, :], xss[:, :], 1.0 / D, EPS, ALU.mult, ALU.add).then_inc(ms_ok, 1)
                    dve.wait_ge(rt_ok, g + 1)
                    ch.link(dve.reciprocal(xrs[:, :], xrt[:, :]))
                    for j in range(4):
                        dve.tensor_scalar(xt[:, j, :], xt[:, j, :], xrs[:, j:j + 1], None,
                                          ALU.mult).then_inc(xn_ok, 1)
                    for k in range(KT):
                        n = g * KT + k
                        dve.wait_ge(xt_mm, n + 1)
                        dve.tensor_scalar(hT[:, k, g * 512:(g + 1) * 512], bank[4 + n % 4][:, :],
                                          gcol[:, k:k + 1], mcol[:, k:k + 1], ALU.mult,
                                          ALU.add).then_inc(h_ok, 1)

            @block.gpsimd
            def _(pool):
                ch = Chain(pool, pch)
                pool.wait_ge(loaded, 16 * 7)
                ch.link(pool.memset(toe[:, :], 0.0))
                ch.link(pool.tensor_scalar(toe[:, 0:512], toe[:, 0:512], relr[:, 0:1], None, ALU.add))
                ch.link(pool.tensor_copy(toe[:, 511:TOE], relr[:, 0:256]))
                ch.link(pool.tensor_scalar(toe[:, :], toe[:, :], 1.0 / SCALE, None, ALU.mult))
                pool.dma_start(toe_d, toe[:, :]).then_inc(toe_out, 16)
                for n in range(NCH):
                    pool.wait_ge(m_add, n + 1)
                    pool.dma_start(mod_d[:, n * 512:(n + 1) * 512], mrow[:, n % 2, :]).then_inc(m_out[n % 2], 16)
                for m in m_out:
                    pool.wait_ge(m, 16 * NCH // 2)
                pool.wait_ge(toe_out, 16)
                pool.wait_ge(trig, 2)


def score_plan(group):
    plan = []
    for t in range(NT):
        k0 = max(0, t - (BAND_T - 1)) if group == "A" else 0
        n = t - k0 + 1
        sizes = [4] * (n // 4) + ([n % 4] if n % 4 else [])
        if n > 4 and sizes[-1] == 1:
            sizes[-2:] = [3, 2]
        pieces = [(k0 + sum(sizes[:i]), m) for i, m in enumerate(sizes)]
        values = pieces
        plan.append((k0, n, pieces, values))
    return plan


def stage2(nc, io, sb, sem, bank, ident, o_d, toe_d, hT, cosT, sinT, rot):
    with ExitStack() as ctx:
        wq = sb(ctx, "wq", [P, KT, P])
        wk = sb(ctx, "wk", [P, KT, P])
        v_all = sb(ctx, "v_all", [P, NT, 512])
        q2 = [sb(ctx, f"q2_{c}", [P, SEQ], F32R) for c in range(2)]
        k_hi = [sb(ctx, f"k_hi{c}", [P, SEQ], F32R) for c in range(2)]
        k_lo = [sb(ctx, f"k_lo{c}", [P, SEQ], F32R) for c in range(2)]
        S0 = sb(ctx, "S0", [P, 2, SEQ])
        S1 = sb(ctx, "S1", [P, SEQ])
        PT = sb(ctx, "PT", [P, 4, 512])
        bias = sb(ctx, "bias", [P, 2, BAND])
        osb = sb(ctx, "osb", [P, 2, P])
        pm = sb(ctx, "pm", [P, 2, 2, 4])
        nm = sb(ctx, "nm", [P, 2, 2])
        l = sb(ctx, "l", [P, 2, 2])
        r = sb(ctx, "r", [P, 2, 2])
        lams = sb(ctx, "lams", [P, 4])
        wv = [S0[:, h, :].rearrange("p (k n) -> p k n", k=KT) for h in range(2)]
        lamv = PT[:, 0, 0:4 * HD].rearrange("p (a d) -> p a d", a=4)
        lamt = PT[:, 1, 0:HD]
        mask = bias[:, 0, :]
        sbank, tbank, obank = bank[0:4], bank[4:6], bank[6:8]
        go = sem("stage2_go")
        sconst = sem("stage2_constants")
        lamch, lam_dots, lam_exp = sem("lambda_chain"), sem("lambda_dots"), sem("lambda_exponentials")

        for group in ("A", "B"):
            A = group == "A"
            plan = score_plan(group)
            NPC = 2 * sum(len(p[2]) for p in plan)
            NVC = (2 if A else 1) * sum(len(p[3]) for p in plan)
            NEV = NVC // 2
            assert NVC % 4 == 0
            q0 = 0 if A else 3 * AW
            k0c = AW if A else 3 * AW + BW
            v0 = 2 * AW if A else 3 * AW + 2 * BW
            s = {n: sem(f"{n}_{group}") for n in (
                "wv_in", "v_mm", "v_ev", "wqk_in", "proj_mm", "proj_ev", "rot_mm", "rot_ok", "bias_in",
                "score_mm", "score_ev", "max_ok", "exp_ok", "val_tr", "ev_act", "ev_dve", "pv_mm",
                "o_ev", "o_out0", "o_out1", "wv_in1", "hi_ok", "lo_ok", "recip_ok", "p1_ok", "comb_ok", "dch", "mask_ok", "rope_done")}
            pc0, vc0 = [0], [0]
            for p in plan:
                pc0.append(pc0[-1] + 2 * len(p[2]))
                vc0.append(vc0[-1] + (2 if A else 1) * len(p[3]))
            OC = 0 if A else AW
            OE = 2 if A else 1

            def val_pieces(t):
                out, i = [], vc0[t]
                for h in range(2 if A else 1):
                    vs = plan[t][3]
                    for j, (kt, n) in enumerate(vs):
                        out.append((i, h, kt, n, j == 0, j == len(vs) - 1))
                        i += 1
                return out

            def scores(b, c):
                if c == 0:
                    return S0[:, b, :]
                return S1[:, b * (SEQ // 2):(b + 1) * (SEQ // 2)] if A else S1[:, :]

            def parts_before(n):
                return 2 * n if n <= 4 else 8 + 4 * (n - 4)

            def parts(n):
                for c in range(2):
                    own, other = slice(c * HD, (c + 1) * HD), slice((1 - c) * HD, (2 - c) * HD)
                    if n < 4:
                        yield q2[c], q2[c], own, own, other
                    else:
                        yield k_hi[c], k_lo[c], own, own, own
                        yield k_hi[c], k_lo[c], own, other, other

            def rotate(pe, u, n):
                pe.wait_ge(s["proj_ev"], 8 * u + n + 1)
                if n >= 2:
                    pe.wait_ge(s["rot_ok"], 8 * u + n - 1)
                else:
                    pe.wait_ge(s["o_ev"], OE * u * NT)
                pe.matmul(obank[n % 2][:, :], rot[:, :], PT[:, n % 2, :],
                          start=True, stop=True).then_inc(s["rot_mm"], 1)

            def values(pe, u, t):
                ps = val_pieces(t)

                def tr(p):
                    i, h, kt, n, first, last = p
                    kk0 = plan[t][0]
                    if A:
                        pe.wait_ge(s["exp_ok"], u * 2 * NT + 2 * t + h + 1)
                    else:
                        pe.wait_ge(s["comb_ok"], u * NT + t + 1)
                    if i >= 2:
                        pe.wait_ge(s["ev_dve"] if i % 2 else s["ev_act"], u * NEV + i // 2)
                    for j in range(n):
                        b = kt - kk0 + j
                        mm = pe.transpose(tbank[i % 2][:, j * P:(j + 1) * P],
                                          scores(t % 2, h)[:, b * P:(b + 1) * P], ident[:, :])
                    mm.then_inc(s["val_tr"], 1)

                def pv(p):
                    i, h, kt, n, first, last = p
                    pe.wait_ge(s["ev_dve"] if i % 2 else s["ev_act"], u * NEV + i // 2 + 1)
                    if first and h == 0:
                        pe.wait_ge(s["o_ev"], OE * (u * NT + max(0, t - 1)))
                    for j in range(n):
                        mm = pe.matmul(obank[t % 2][:, h * P:(h + 1) * P], PT[:, i % 4, j * P:(j + 1) * P],
                                       v_all[:, kt + j, bass.ds(u * P, P)],
                                       start=(first and j == 0), stop=(last and j == n - 1))
                    mm.then_inc(s["pv_mm"], 1)

                for j, p in enumerate(ps):
                    tr(p)
                    if j:
                        pv(ps[j - 1])
                pv(ps[-1])

            def evacuate(eng, done, u, i, n):
                if i >= 4:
                    eng.wait_ge(s["pv_mm"], u * NVC + i - 3)
                eng.wait_ge(s["val_tr"], u * NVC + i + 1)
                src, dst = tbank[i % 2][:, 0:n * P], PT[:, i % 4, 0:n * P]
                if i % 2:
                    eng.tensor_copy(dst, src).then_inc(done, 1)
                else:
                    eng.activation(dst, src, ACT.Copy).then_inc(done, 1)

            def output(dve, u, t, ch):
                b = t % 2
                dve.wait_ge(s["pv_mm"], u * NVC + vc0[t + 1])
                out_slot_free(dve, u, t)
                if A:
                    for h in range(2):
                        dve.tensor_scalar(osb[:, t % 2, h * HD:(h + 1) * HD],
                                          obank[b][:, h * (P + HD):h * (P + HD) + HD], r[:, b, h:h + 1], None,
                                          ALU.mult).then_inc(s["o_ev"], 1)
                else:
                    dve.tensor_copy(osb[:, t % 2, :], obank[b][:, 0:P]).then_inc(s["o_ev"], 1)

            def out_slot_free(dve, u, t):
                dve.wait_ge(s[f"o_out{t % 2}"], 8 * NT * u + 16 * (t // 2))

            with nc.Block() as block:
                @block.sync
                def _(sp):
                    if not A:
                        sp.dma_start(lamv, io["lambdas"].rearrange("(o a) d -> o a d", o=1)
                                     .broadcast_to([P, 4, HD])).then_inc(sconst, 16)

                    def load_qk(u):
                        sp.dma_start(wq[:, :, :], io["w_in"][:, bass.ds(q0 + u * P, P)]
                                     .rearrange("(k p) n -> p k n", p=P)).then_inc(s["wqk_in"], 16)
                        sp.dma_start(wk[:, :, :], io["w_in"][:, bass.ds(k0c + u * P, P)]
                                     .rearrange("(k p) n -> p k n", p=P)).then_inc(s["wqk_in"], 16)

                    for h in range(2):
                        sp.dma_start(wv[h], io["w_in"][:, v0 + 256 * h:v0 + 256 * (h + 1)]
                                     .rearrange("(k p) n -> p k n", p=P)).then_inc(s["wv_in1" if h else "wv_in"], 16)
                        if h == 0:
                            load_qk(0)

                    def unit(u, last):
                        if A:
                            sp.wait_ge(s["score_ev"], u * NPC)
                            for h in range(2):
                                src = bass.AP(io["bias_scratch"].tensor, (2 * u + h) * (P * TOE) + P - 1,
                                              [[TOE - 1, P], [1, BAND]])
                                sp.dma_start(bias[:, h, :], src).then_inc(s["bias_in"], 16)
                        if not last:
                            sp.wait_ge(s["proj_mm"], u * 8 + 8)
                            load_qk(u + 1)
                        for t in range(NT):
                            sp.wait_ge(s["o_ev"], OE * (u * NT + t + 1))
                            sp.dma_start(o_d[t * P:(t + 1) * P, bass.ds(OC + u * P, P)],
                                         osb[:, t % 2, :]).then_inc(s[f"o_out{t % 2}"], 16)
                    with sp.Fori(0, UNITS - 1) as u:
                        unit(u, False)
                    unit(UNITS - 1, True)
                    for j in range(2):
                        sp.wait_ge(s[f"o_out{j}"], 8 * NT * UNITS)

                @block.tensor
                def _(pe):
                    for h in range(2):
                        pe.wait_ge(s["wv_in1" if h else "wv_in"], 16)
                        for t in range(NT):
                            n = h * NT + t
                            if n >= 2:
                                pe.wait_ge(s["v_ev"], n - 1)
                            for k in range(KT):
                                mm = pe.matmul(tbank[n % 2][:, 0:256], hT[:, k, t * P:(t + 1) * P],
                                               wv[h][:, k, :], start=(k == 0), stop=(k == KT - 1))
                            mm.then_inc(s["v_mm"], 1)
                    pe.wait_ge(s["v_ev"], 2 * NT)
                    with pe.Fori(0, UNITS) as u:
                        pe.wait_ge(s["wqk_in"], 32 * u + 32)
                        for n in range(8):
                            w = wq if n < 4 else wk
                            g = n % 4
                            if n >= 2:
                                pe.wait_ge(s["proj_ev"], 8 * u + n - 1)
                            for k in range(KT):
                                mm = pe.matmul(tbank[n % 2][:, :], w[:, k, :], hT[:, k, g * 512:(g + 1) * 512],
                                               start=(k == 0), stop=(k == KT - 1))
                            mm.then_inc(s["proj_mm"], 1)
                            if not A and n >= 1:
                                rotate(pe, u, n - 1)
                        if not A:
                            rotate(pe, u, 7)
                        pe.wait_ge(s["lo_ok"], 24 * (u + 1))
                        for step in range(NT + 1):
                            if step < NT:
                                i = pc0[step]
                                for c in range(2):
                                    for kt, n in plan[step][2]:
                                        if i >= 4:
                                            pe.wait_ge(s["score_ev"], u * NPC + i - 3)
                                        for part in (k_hi[c], k_lo[c]):
                                            mm = pe.matmul(sbank[i % 4][:, 0:n * P],
                                                           q2[c][:, step * P:(step + 1) * P],
                                                           part[:, kt * P:(kt + n) * P],
                                                           start=part is k_hi[c], stop=part is k_lo[c])
                                        mm.then_inc(s["score_mm"], 1)
                                        i += 1
                            if step >= 1:
                                values(pe, u, step - 1)

                @block.scalar
                def _(act):
                    if not A:
                        act.wait_ge(lam_dots, 1)
                        act.activation(lams[:, 0:2], lams[:, 0:2], ACT.Exp).then_inc(lam_exp, 1)
                    for n in range(2 * NT):
                        h, t = n // NT, n % NT
                        act.wait_ge(s["v_mm"], n + 1)
                        act.activation(v_all[:, t, 256 * h:256 * (h + 1)], tbank[n % 2][:, 0:256],
                                       ACT.Copy).then_inc(s["v_ev"], 1)
                    with act.Fori(0, UNITS) as u:
                        for n in range(9):
                            if n < 8:
                                if n >= 2:
                                    act.wait_ge(s["lo_ok"], 24 * u + parts_before(n - 1))
                                act.wait_ge(s["proj_mm"], 8 * u + n + 1)
                                act.activation(PT[:, n % 2, :], tbank[n % 2][:, :], ACT.Copy).then_inc(s["proj_ev"], 1)
                            if n >= 1:
                                m = n - 1
                                cols = slice(m % 4 * 512, (m % 4 + 1) * 512)
                                act.wait_ge(s["proj_ev" if A else "rope_done"], 8 * u + m + 1)
                                for hi, lo, src, to, _to in parts(m):
                                    act.activation(hi[to, cols], PT[src, m % 2, :], ACT.Copy).then_inc(s["hi_ok"], 1)
                        for step in range(NT + 1):
                            if step < NT:
                                n = plan[step][1] * P
                                for c in range(2):
                                    act.wait_ge(s["max_ok"], u * 2 * NT + 2 * step + c + 1)
                                    act.activation(scores(step % 2, c)[:, 0:n], scores(step % 2, c)[:, 0:n], ACT.Exp,
                                                   bias=nm[:, step % 2, c:c + 1],
                                                   accum_out=l[:, step % 2, c:c + 1]).then_inc(s["exp_ok"], 1)
                            if step >= 1:
                                for i, h, kt, n, first, last in val_pieces(step - 1):
                                    if i % 2 == 0:
                                        evacuate(act, s["ev_act"], u, i, n)
                            if step < NT and not A:
                                n = plan[step][1] * P
                                act.wait_ge(s["recip_ok"], u * NT + step + 1)
                                act.activation(scores(step % 2, 1)[:, 0:n], scores(step % 2, 1)[:, 0:n], ACT.Copy,
                                               scale=r[:, step % 2, 1:2]).then_inc(s["p1_ok"], 1)

                @block.gpsimd
                def _(pool):
                    if A:
                        pool.sem_inc(go, 1)
                        with pool.Fori(0, UNITS) as u:
                            hold(pool, go, (s["bias_in"], 32 * u + 32))
                            pool.memset(bias[0:HD, :, BAND - HD:BAND], NEG * 8).then_inc(s["mask_ok"], 1)
                            pool.memset(bias[HD:P, :, 0:HD], NEG * 8).then_inc(s["mask_ok"], 1)
                    else:
                        pool.memset(mask, 0.0).then_inc(s["mask_ok"], 1)
                        pool.wait_ge(s["mask_ok"], 1)
                        pool.memset(mask[0:HD, BAND - HD:BAND], NEG * 8).then_inc(s["mask_ok"], 1)

                @block.vector
                def _(dve):
                    if not A:
                        ch = Chain(dve, lamch)
                        dve.wait_ge(sconst, 16)
                        ch.link(dve.tensor_tensor_reduce(lamt, lamv[:, 0, :], lamv[:, 1, :], 1.0, 0.0,
                                                         ALU.mult, ALU.add, lams[:, 0:1]))
                        ch.link(dve.tensor_tensor_reduce(lamt, lamv[:, 2, :], lamv[:, 3, :], 1.0, 0.0,
                                                         ALU.mult, ALU.add, lams[:, 1:2]))
                        dve.sem_inc(lam_dots, 1)
                        dve.wait_ge(lam_exp, 1)
                        ch.link(dve.tensor_tensor(lams[:, 2:3], lams[:, 1:2], lams[:, 0:1], ALU.subtract))
                        ch.link(dve.tensor_scalar(lams[:, 2:3], lams[:, 2:3], -LAM0, None, ALU.add))
                        dve.wait_ge(s["mask_ok"], 2)
                    PER = NT if A else NT + 8
                    with dve.Fori(0, UNITS) as u:
                        ch = Chain(dve, s["dch"], u * PER)
                        for n in range(8):
                            cols = slice(n % 4 * 512, (n % 4 + 1) * 512)
                            raw, tmp = PT[:, n % 2, :], PT[:, 2 + n % 2, :]
                            if not A:
                                dve.wait_ge(s["rot_mm"], 8 * u + n + 1)
                                dve.tensor_tensor(tmp, obank[n % 2][:, :], sinT[:, cols], ALU.mult).then_inc(s["rot_ok"], 1)
                                ch.link(dve.tensor_tensor(raw, raw, cosT[:, cols], ALU.mult))
                                dve.wait_ge(s["rot_ok"], 8 * u + n + 1)
                                dve.tensor_tensor(raw, raw, tmp, ALU.add).then_inc(s["rope_done"], 1)
                            dve.wait_ge(s["hi_ok"], 24 * u + parts_before(n + 1))
                            for hi, lo, src, _to, to in parts(n):
                                dve.tensor_tensor(lo[to, cols], PT[src, n % 2, :], hi[src, cols].bitcast(F32),
                                                  ALU.subtract).then_inc(s["lo_ok"], 1)
                        if A:
                            hold(dve, go, (s["mask_ok"], 2 * u + 2))
                        for step in range(NT + 1):
                            if step < NT:
                                b = step % 2
                                k0, nt, pieces, _v = plan[step]
                                i = pc0[step]
                                if step >= 2:
                                    hold(dve, go, (s["val_tr"], u * NVC + vc0[step - 1]))
                                for c in range(2):
                                    for j, (kt, n) in enumerate(pieces):
                                        hold(dve, go, (s["score_mm"], u * NPC + i + 1))
                                        if A:
                                            o = (kt - (step - 4)) * P
                                            add = bias[:, c, o:o + n * P]
                                        elif kt + n == step + 1:
                                            add = mask[:, BAND - n * P:BAND]
                                        else:
                                            add = mask[:, 0:n * P]
                                        cs = (kt - k0) * P
                                        dve.tensor_tensor_reduce(
                                            scores(b, c)[:, cs:cs + n * P], sbank[i % 4][:, 0:n * P], add,
                                            SCALE, NEG * 8, ALU.add, ALU.max,
                                            pm[:, b, c, j:j + 1]).then_inc(s["score_ev"], 1)
                                        i += 1
                                    dve.wait_ge(s["score_ev"], u * NPC + i)
                                    dve.tensor_reduce(nm[:, b, c:c + 1], pm[:, b, c, 0:len(pieces)], AX,
                                                      ALU.max, negate=True).then_inc(s["max_ok"], 1)
                            if step >= 1:
                                t = step - 1
                                for i, h, kt, n, first, last in val_pieces(t):
                                    if i % 2:
                                        evacuate(dve, s["ev_dve"], u, i, n)
                                output(dve, u, t, ch)
                            if step < NT:
                                b = step % 2
                                dve.wait_ge(s["exp_ok"], u * 2 * NT + 2 * step + 2)
                                m = ch.add(dve.reciprocal(r[:, b, :], l[:, b, :]))
                                hold(dve, go, (s["dch"], m))
                                if not A:
                                    dve.tensor_scalar(r[:, b, 1:2], r[:, b, 1:2], lams[:, 2:3], None,
                                                      ALU.mult).then_inc(s["recip_ok"], 1)
                                    n = plan[step][1] * P
                                    dve.wait_ge(s["p1_ok"], u * NT + step + 1)
                                    dve.scalar_tensor_tensor(S0[:, b, 0:n], S0[:, b, 0:n], r[:, b, 0:1],
                                                             S1[:, 0:n], ALU.mult, ALU.add).then_inc(s["comb_ok"], 1)
                        assert ch.n == PER, (group, ch.n)



def pipelined(eng, step):
    for t in (-1, 0, 1, 2):
        step(t, t % 2, True, t >= 0, t >= 1, t >= 2)
    with eng.Fori(2, NT // 2) as i:
        step(2 * i - 1, 1, True, True, True, True)
        step(2 * i, 0, True, True, True, True)
    step(NT - 1, 1, False, True, True, True)
    step(NT, 0, False, False, True, True)
    step(NT + 1, 1, False, False, False, True)


def half(t):
    return t // 2


def wait(eng, sem, value):
    if not (isinstance(value, int) and value <= 0):
        eng.wait_ge(sem, value)


def stage3(nc, io, sb, sem, bank, ident, mod_d, o_d, acc_d, h2_d, list_d, table):
    with ExitStack() as ctx:
        wout = sb(ctx, "wout", [P, KT, D])
        gtm = sb(ctx, "gtm", [P, D])
        g2 = sb(ctx, "g2", [P, D])
        g2s = sb(ctx, "g2s", [P, D])
        sh2 = sb(ctx, "sh2", [P, D])
        wr = sb(ctx, "wr", [P, KT, NE])
        br = sb(ctx, "br", [P, NE])
        ot = sb(ctx, "ot", [P, 2, D])
        xt = sb(ctx, "xt3", [P, 2, D])
        oT = sb(ctx, "oT", [P, 2, KT, P])
        h2 = sb(ctx, "h2", [P, 2, D])
        h2T = sb(ctx, "h2T", [P, 2, KT, P])
        sq = sb(ctx, "sq3", [P, D])
        tmp = sb(ctx, "tmp3", [P, 2, 512])
        st = sb(ctx, "st3", [P, 4])
        hs = sb(ctx, "hs", [P, 5, B_HEADS])
        osq = sb(ctx, "osq3", [P, 2, B_HEADS, P])
        gsub = sb(ctx, "gsub", [P, P])
        tri = sb(ctx, "tri", [P, P])
        ones = sb(ctx, "ones", [P, P])
        iota = sb(ctx, "iota_e", [P, NE])
        eoff = sb(ctx, "eoff", [P, NE])
        tokc = sb(ctx, "tokc", [P, 1])
        lg = sb(ctx, "lg", [P, 2, NE])
        v8 = sb(ctx, "v8", [P, 2, 8])
        i8 = sb(ctx, "i8", [P, 2, 8], U32)
        i4 = sb(ctx, "i4", [P, 2, TOPK])
        nv = sb(ctx, "nv", [P, 2])
        ex = sb(ctx, "ex", [P, 2, TOPK])
        es = sb(ctx, "es", [P, 2])
        oh = sb(ctx, "oh", [P, 2, TOPK, NE])
        M = sb(ctx, "M", [P, 2, NE])
        macc = sb(ctx, "macc", [P, NE])
        base = sb(ctx, "base", [P, 2, NE])
        ohs = sb(ctx, "ohs", [P, TOPK, NE])
        slotf = sb(ctx, "slotf", [P, 2, TOPK])
        slot = sb(ctx, "slot", [P, 2, TOPK], I32)
        pay = sb(ctx, "pay", [P, 2, TOPK, 2])
        padl = sb(ctx, "padl", [P, CAP * NE // P, 2])
        cnt = sb(ctx, "cnt", [P, 4, NE])
        cnti = sb(ctx, "cnti", [P, NE], I32)

        (go, cin, win, oT_mm, oT_ev, mix_mm, x1_ok, sq_ok, h2_ok, hT_mm, hT_ev, lg_mm, lg_ok,
         ex_ok, nv_ok, oh_ok, rk_mm, macc_ok, slot_ok, pads, pch, pref, ini, chf, chm,
         chb, che, cmm, tab_ok, on_ok, ms_ok, rt_ok, oms_ok, ort_ok, che1) = (sem(f"s3_{n}") for n in (
            "go", "constants_in", "weights_in", "oT_product", "oT_copied", "mix_product",
            "x1_ready", "squares_summed", "h2_ready", "h2T_product", "h2T_copied", "logits_product",
            "logits_copied", "exponentials", "max_negated", "onehots_ready", "ranks_product", "counts_added",
            "slots_ready", "pads_ready", "pool_chain", "prefilled",
            "vector_constants", "front_chain", "middle_chain", "back_chain", "end_chain", "counts_product",
            "table_ready", "heads_normalised", "mean_square", "root", "heads_mean_square", "heads_root",
            "early_chain"))
        o_in, x_in, acc_out, h2_out, scat = (
            [sem(f"s3_{n}{i}") for i in range(2)] for n in ("o_in", "x_in", "acc_stored", "h2_stored", "scattered"))
        NEARLY, NF, NM, NB = 7, 4, 5, 6

        with nc.Block() as block:
            @block.sync
            def _(sp):
                sp.dma_start(wout[:, :, :], io["w_out"].rearrange("(k p) n -> p k n", p=P)).then_inc(win, 16)
                for dst, src in ((gtm, mod_d[:, 2 * D:3 * D]), (sh2, mod_d[:, 3 * D:4 * D]),
                                 (g2s, mod_d[:, 4 * D:5 * D]), (g2, io["g_ffn_norm"])):
                    sp.dma_start(dst[:, :], src.broadcast_to([P, D])).then_inc(cin, 16)
                sp.dma_start(gsub[:, :], io["g_subln"].broadcast_to([P, P])).then_inc(cin, 16)
                sp.dma_start(br[:, :], io["b_router"].broadcast_to([P, NE])).then_inc(cin, 16)
                sp.dma_start(iota[:, :], io["iota_e"].broadcast_to([P, NE])).then_inc(cin, 16)
                sp.dma_start(eoff[:, :], io["expert_offset"].broadcast_to([P, NE])).then_inc(cin, 16)
                sp.dma_start(tri[:, :], io["tri"]).then_inc(cin, 16)
                sp.dma_start(tokc[:, :], io["partition_index"]).then_inc(cin, 16)
                sp.dma_start(wr[:, :, :], io["w_router"].rearrange("(k p) n -> p k n", p=P)).then_inc(cin, 16)

                def step(t, b, early, front, middle, back):
                    if early:
                        wait(sp, oT_mm, 2 * t)
                        sp.dma_start(ot[:, 1 - b, :], o_d[bass.ds((t + 1) * P, P), :]).then_inc(o_in[1 - b], 16)
                        wait(sp, acc_out[1 - b], 16 * half(t + 1 - (1 - b)))
                        wait(sp, h2_ok, t)
                        sp.dma_start(xt[:, 1 - b, :], io["x"][bass.ds((t + 1) * P, P), :]).then_inc(x_in[1 - b], 16)
                pipelined(sp, step)

            @block.tensor
            def _(pe):
                pe.wait_ge(cin, 176)
                pe.wait_ge(ini, 3)

                def step(t, b, early, front, middle, back):
                    if front:
                        pe.wait_ge(o_in[b], 16 * half(t - b) + 16)
                        pe.wait_ge(on_ok, B_HEADS * (t + 1))
                        for h in range(2):
                            wait(pe, oT_ev, 2 * t - 1 + h)
                            for j in range(4):
                                k = 4 * h + j
                                mm = pe.transpose(bank[h][:, j * P:(j + 1) * P], ot[:, b, k * P:(k + 1) * P],
                                                  ident[:, :])
                            mm.then_inc(oT_mm, 1)
                        pe.wait_ge(oT_ev, 2 * t + 2)
                        pe.wait_ge(win, 16)
                        for h in range(2):
                            wait(pe, x1_ok, 2 * t - 1 + h)
                            for k in range(KT):
                                mm = pe.matmul(bank[2 + h][:, :], oT[:, b, k, :], wout[:, k, h * 512:(h + 1) * 512],
                                               start=(k == 0), stop=(k == KT - 1))
                            mm.then_inc(mix_mm, 1)
                    if middle:
                        c, tm = 1 - b, t - 1
                        pe.wait_ge(h2_ok, tm + 1)
                        for h in range(2):
                            wait(pe, hT_ev, 2 * tm - 1 + h)
                            for j in range(4):
                                k = 4 * h + j
                                mm = pe.transpose(bank[4 + h][:, j * P:(j + 1) * P], h2[:, c, k * P:(k + 1) * P],
                                                  ident[:, :])
                            mm.then_inc(hT_mm, 1)
                        pe.wait_ge(hT_ev, 2 * tm + 2)
                        wait(pe, lg_ok, tm)
                        for k in range(KT):
                            mm = pe.matmul(bank[6][:, 0:NE], h2T[:, c, k, :], wr[:, k, :],
                                           start=(k == 0), stop=(k == KT - 1))
                        mm.then_inc(lg_mm, 1)
                    if back:
                        tb = t - 2
                        pe.wait_ge(oh_ok, tb + 1)
                        pe.wait_ge(macc_ok, tb + 1)
                        pe.matmul(bank[7][:, 0:NE], tri[:, :], M[:, b, :], start=True, stop=False)
                        pe.matmul(bank[7][:, 0:NE], ones[:, :], macc[:, :], start=False,
                                  stop=True).then_inc(rk_mm, 1)
                pipelined(pe, step)
                pe.wait_ge(macc_ok, NT + 1)
                pe.matmul(bank[7][:, 0:NE], ones[:, :], macc[:, :], start=True, stop=True).then_inc(cmm, 1)

            @block.scalar
            def _(act):
                def step(t, b, early, front, middle, back):
                    if front:
                        for h in range(2):
                            act.wait_ge(oT_mm, 2 * t + 1 + h)
                            wait(act, mix_mm, 2 * (t - 1))
                            act.activation(oT[:, b, 4 * h:4 * h + 4, :].rearrange("p a b -> p (a b)"),
                                           bank[h][:, :], ACT.Copy).then_inc(oT_ev, 1)
                    if early:
                        act.wait_ge(oms_ok, t + 2)
                        act.activation(hs[:, 2, :], hs[:, 1, :], ACT.Sqrt).then_inc(ort_ok, 1)
                    if front:
                        act.wait_ge(x1_ok, 2 * t + 2)
                        wait(act, h2_ok, t)
                        act.activation(sq[:, :], xt[:, b, :], ACT.Square, accum_out=st[:, 0:1]).then_inc(sq_ok, 1)
                        act.wait_ge(ms_ok, t + 1)
                        act.activation(st[:, 2:3], st[:, 1:2], ACT.Sqrt).then_inc(rt_ok, 1)
                    if middle:
                        c, tm = 1 - b, t - 1
                        for h in range(2):
                            act.wait_ge(hT_mm, 2 * tm + 1 + h)
                            wait(act, lg_mm, tm - 1)
                            act.activation(h2T[:, c, 4 * h:4 * h + 4, :].rearrange("p a b -> p (a b)"),
                                           bank[4 + h][:, :], ACT.Copy).then_inc(hT_ev, 1)
                        act.wait_ge(nv_ok, tm + 1)
                        act.activation(ex[:, c, :], v8[:, c, 0:TOPK], ACT.Exp, bias=nv[:, c:c + 1],
                                       accum_out=es[:, c:c + 1]).then_inc(ex_ok, 1)
                pipelined(act, step)

            @block.gpsimd
            def _(pool):
                ch = Chain(pool, pch)
                padi = padl[:, :, :].bitcast(I32)
                ch.link(pool.memset(padl[:, :, :], 0.0))
                pool.iota(padi[:, :, 0].rearrange("p (a b) -> p a b", b=P), [[0, CAP * NE // P // P], [1, P]],
                          base=SEQ, channel_multiplier=0).then_inc(pads, 1)
                ch.link(pool.memset(sq[:, :], 0.0))
                pool.dma_start(acc_d[SEQ:ROWS, :], sq[:, :]).then_inc(pref, 16)
                pool.dma_start(h2_d[SEQ:ROWS, :], sq[:, :]).then_inc(pref, 16)
                pool.wait_ge(pads, 1)
                pool.dma_start(list_d.rearrange("(p a) b -> p a b", p=P), padl[:, :, :]).then_inc(pref, 16)
                pool.wait_ge(pref, 48)
                pool.sem_inc(go, 1)

                def step(t, b, early, front, middle, back):
                    if front:
                        hold(pool, go, (x1_ok, 2 * t + 2))
                        pool.dma_start(acc_d[bass.ds(t * P, P), :], xt[:, b, :]).then_inc(acc_out[b], 16)
                        hold(pool, go, (h2_ok, t + 1))
                        pool.dma_start(h2_d[bass.ds(t * P, P), :], h2[:, b, :]).then_inc(h2_out[b], 16)
                    if back:
                        tb = t - 2
                        hold(pool, go, (slot_ok, tb + 1))
                        for k in range(TOPK):
                            pool.indirect_dma_start(
                                list_d, bass.IndirectOffsetOnAxis(ap=slot[:, b, k:k + 1], axis=0),
                                pay[:, b, k, :], None).then_inc(scat[b], 16)
                pipelined(pool, step)
                for b in range(2):
                    pool.wait_ge(acc_out[b], 8 * NT)
                    pool.wait_ge(h2_out[b], 8 * NT)
                    pool.wait_ge(scat[b], 8 * NT * TOPK)

            @block.vector
            def _(dve):
                dve.wait_ge(cin, 176)
                dve.memset(ones[:, :], 1.0).then_inc(ini, 1)
                dve.memset(macc[:, :], 0.0).then_inc(ini, 1)
                dve.sem_inc(macc_ok, 1)
                dve.tensor_scalar(g2s[:, :], g2s[:, :], 1.0, None, ALU.add).then_inc(ini, 1)
                dve.wait_ge(ini, 3)
                dve.tensor_tensor(g2[:, :], g2[:, :], g2s[:, :], ALU.mult).then_inc(ini, 1)
                dve.tensor_scalar(gsub[:, :], gsub[:, :], 1.0 - LAM0, None, ALU.mult).then_inc(ini, 1)
                dve.wait_ge(ini, 5)
                dve.wait_ge(pref, 48)

                def step(t, b, early, front, middle, back):
                    if early:
                        ch = Chain(dve, che1, (t + 1) * NEARLY)
                        c = 1 - b
                        dve.wait_ge(o_in[c], 16 * half(t + 1 - c) + 16)
                        heads = ot[:, c, AW:D].rearrange("p (h d) -> p h d", h=B_HEADS)
                        ch.link(dve.tensor_scalar(osq[:, 0, :, :], heads, -2.0 ** 100, 2.0 ** 100, ALU.max, ALU.min))
                        ch.link(dve.scalar_tensor_tensor(osq[:, 1, :, :], osq[:, 0, :, :], 2.0 ** -80,
                                                         osq[:, 0, :, :], ALU.mult, ALU.mult))
                        ch.link(dve.tensor_reduce(hs[:, 0, :], osq[:, 1, :, :], AX, ALU.add))
                        ch.link(dve.tensor_scalar(hs[:, 3, :], hs[:, 0, :], 2.0 ** 48, 2.0 ** -40, ALU.is_le, ALU.mult))
                        ch.link(dve.tensor_scalar(hs[:, 1, :], hs[:, 0, :], 1.0 / P, EPS * 2.0 ** -80, ALU.mult, ALU.add))
                        dve.tensor_scalar(hs[:, 1, :], hs[:, 1, :], 2.0 ** 100, None, ALU.min).then_inc(oms_ok, 1)
                        dve.wait_ge(ort_ok, t + 2)
                        ch.link(dve.reciprocal(hs[:, 4, :], hs[:, 2, :]))
                        ch.link(dve.tensor_tensor(hs[:, 4, :], hs[:, 4, :], hs[:, 3, :], ALU.mult))
                        for h in range(B_HEADS):
                            dve.scalar_tensor_tensor(heads[:, h, :], heads[:, h, :], hs[:, 4, h:h + 1], gsub[:, :],
                                                     ALU.mult, ALU.mult).then_inc(on_ok, 1)
                        assert ch.n == NEARLY
                    if front:
                        ch = Chain(dve, chf, t * NF)
                        dve.wait_ge(x_in[b], 16 * half(t - b) + 16)
                        for h in range(2):
                            cs = slice(h * 512, (h + 1) * 512)
                            dve.wait_ge(mix_mm, 2 * t + 1 + h)
                            ch.link(dve.tensor_tensor(tmp[:, h, :], bank[2 + h][:, :], gtm[:, cs], ALU.mult))
                            dve.tensor_tensor(xt[:, b, cs], xt[:, b, cs], tmp[:, h, :], ALU.add).then_inc(x1_ok, 1)
                        dve.wait_ge(sq_ok, t + 1)
                        dve.tensor_scalar(st[:, 1:2], st[:, 0:1], 1.0 / D, EPS, ALU.mult, ALU.add).then_inc(ms_ok, 1)
                        dve.wait_ge(rt_ok, t + 1)
                        ch.link(dve.reciprocal(st[:, 3:4], st[:, 2:3]))
                        wait(dve, h2_out[b], 16 * half(t - b))
                        wait(dve, hT_mm, 2 * (t - 1))
                        ch.link(dve.scalar_tensor_tensor(h2[:, b, :], xt[:, b, :], st[:, 3:4], g2[:, :],
                                                         ALU.mult, ALU.mult))
                        dve.tensor_tensor(h2[:, b, :], h2[:, b, :], sh2[:, :], ALU.add).then_inc(h2_ok, 1)
                        assert ch.n == NF
                    if middle:
                        c, tm = 1 - b, t - 1
                        ch = Chain(dve, chm, tm * NM)
                        dve.wait_ge(lg_mm, tm + 1)
                        dve.tensor_tensor(lg[:, c, :], bank[6][:, 0:NE], br[:, :], ALU.add).then_inc(lg_ok, 1)
                        hold(dve, ini, (lg_ok, tm + 1))
                        m = ch.add(dve.max(v8[:, c, :], lg[:, c, :]))
                        hold(dve, ini, (chm, m))
                        ch.link(dve.max_index(i8[:, c, :], v8[:, c, :], lg[:, c, :]))
                        dve.tensor_scalar(nv[:, c:c + 1], v8[:, c, 0:1], -1.0, None, ALU.mult).then_inc(nv_ok, 1)
                        ch.link(dve.tensor_copy(i4[:, c, :], i8[:, c, 0:TOPK]))
                        for k in range(TOPK):
                            ins = dve.tensor_scalar(oh[:, c, k, :], iota[:, :], i4[:, c, k:k + 1], None,
                                                    ALU.is_equal)
                        ch.link(ins)
                        dve.tensor_reduce(M[:, c, :], oh[:, c, :, :].rearrange("p k e -> p e k"), AX,
                                          ALU.add).then_inc(oh_ok, 1)
                        dve.wait_ge(ex_ok, tm + 1)
                        ch.link(dve.reciprocal(es[:, c:c + 1], es[:, c:c + 1]))
                        assert ch.n == NM
                    if back:
                        tb = t - 2
                        ch = Chain(dve, chb, tb * NB)
                        wait(dve, scat[b], 16 * TOPK * half(tb - b))
                        dve.wait_ge(rk_mm, tb + 1)
                        dve.tensor_scalar(pay[:, b, :, 1], ex[:, b, :], es[:, b:b + 1], None, ALU.mult)
                        dve.tensor_copy(pay[:, b, :, 0].bitcast(I32), tokc[:, 0:1].broadcast_to([P, TOPK]))
                        ch.link(dve.tensor_tensor(base[:, b, :], bank[7][:, 0:NE], eoff[:, :], ALU.add))
                        ch.link(dve.tensor_scalar(tokc[:, :], tokc[:, :], float(P), None, ALU.add))
                        dve.tensor_tensor(macc[:, :], macc[:, :], M[:, b, :], ALU.add).then_inc(macc_ok, 1)
                        for k in range(TOPK):
                            ch.link(dve.tensor_tensor_reduce(ohs[:, k, :], oh[:, b, k, :], base[:, b, :], 1.0, 0.0,
                                                             ALU.mult, ALU.add, slotf[:, b, k:k + 1]))
                        dve.tensor_copy(slot[:, b, :], slotf[:, b, :]).then_inc(slot_ok, 1)
                        assert ch.n == NB
                pipelined(dve, step)
                ch = Chain(dve, che)
                dve.wait_ge(cmm, 1)
                ch.link(dve.tensor_scalar(cnt[:, 0, :], bank[7][:, 0:NE], float(P - 1), None, ALU.add))
                ch.link(dve.tensor_copy(cnti[:, :], cnt[:, 0, :]))
                ch.link(dve.tensor_scalar(cnti[:, :], cnti[:, :], 7, None, ALU.arith_shift_right))
                ch.link(dve.tensor_copy(cnt[:, 1, :], cnti[:, :]))
                ch.link(dve.tensor_scalar(cnt[:, 1, :], cnt[:, 1, :], 1.0, None, ALU.max))
                ch.link(dve.tensor_tensor_scan(cnt[:, 2, :], ones[:, 0:NE], cnt[:, 1, :], 0.0, ALU.mult, ALU.add))
                ch.link(dve.tensor_tensor(cnt[:, 3, :], cnt[:, 2, :], cnt[:, 1, :], ALU.subtract))
                ch.link(dve.tensor_copy(table[0:1, 0:NE], cnt[0:1, 1, :]))
                ch.link(dve.tensor_copy(table[0:1, NE:2 * NE], cnt[0:1, 3, :]))
                ch.link(dve.tensor_copy(table[0:1, 2 * NE:2 * NE + 1], cnt[0:1, 2, NE - 1:NE]))


def stage4(nc, io, sb, sem, bank, ident, mod_d, acc_d, h2_d, list_d, table):
    with ExitStack() as ctx:
        wgu = sb(ctx, "wgu", [P, 2, KT, 2 * D])
        wd = sb(ctx, "wd", [P, KT, D])
        bgu = sb(ctx, "bgu", [P, 2 * D])
        bd = sb(ctx, "bd", [P, D])
        gtf = sb(ctx, "gtf", [P, D])
        xg = sb(ctx, "xg", [P, D])
        xT = sb(ctx, "xT", [P, KT, P])
        gate = sb(ctx, "gate", [P, 512])
        sig = sb(ctx, "sig", [P, 512])
        up = sb(ctx, "up", [P, 512])
        a = sb(ctx, "a", [P, D])
        aT = sb(ctx, "aT", [P, KT, P])
        y = sb(ctx, "y", [P, D])
        idn = sb(ctx, "idn", [P, 2])
        idc = sb(ctx, "idc", [P, 2])
        pidx = sb(ctx, "pidx", [P, 1])

        (go, cin, wd_in, bg_in, bd_in, gu_mm, g_ev, tx_mm, tx_ev, a_ok, ta_mm, ta_ev, y_mm, y_ok,
         li, xg_in, sc, idc_ok, sig_ok, gate_ok, gch, pch, tab) = (sem(f"s4_{n}") for n in (
            "go", "constants_in", "down_in", "bias_gu_in", "bias_d_in", "gate_up_product",
            "gate_up_read", "x_transposed", "xT_copied", "act_ready", "act_transposed", "aT_copied",
            "down_product", "y_ready", "list_in", "rows_gathered", "scattered", "ids_current",
            "sigmoid_ready", "gate_ready", "vector_chain", "pool_chain", "tab"))
        gu_in = [sem(f"s4_gate_up_in{i}") for i in range(2)]
        NG = 6

        def expert_tiles(eng, e):
            n = eng.value_load(table[0:1, bass.ds(e, 1)], min_val=1, max_val=CAP // P)
            b = eng.value_load(table[0:1, bass.ds(e + NE, 1)], min_val=0, max_val=TOPK * NT + NE)
            return n, b

        with nc.Block() as block:
            @block.sync
            def _(sp):
                sp.dma_start(gtf[:, :], mod_d[:, 5 * D:6 * D].broadcast_to([P, D])).then_inc(cin, 16)
                sp.dma_start(pidx[:, :], io["partition_index"]).then_inc(cin, 16)

                def load_gu(e, b):
                    sp.dma_start(wgu[:, b, :, :], io["w_gate_up"][bass.ds(e, 1), :, :]
                                 .rearrange("o (k p) n -> p (o k) n", p=P)).then_inc(gu_in[b], 16)

                def load_down(e):
                    before = sp.value_load(table[0:1, bass.ds(e + NE, 1)], min_val=0, max_val=TOPK * NT + NE)
                    sp.wait_ge(g_ev, 4 * before)
                    sp.dma_start(bgu[:, :], io["b_gate_up"][bass.ds(e, 1), :].broadcast_to([P, 2 * D])).then_inc(bg_in, 16)
                    sp.wait_ge(y_mm, 2 * before)
                    sp.dma_start(wd[:, :, :], io["w_down"][bass.ds(e, 1), :, :]
                                 .rearrange("o (k p) n -> p (o k) n", p=P)).then_inc(wd_in, 16)
                    sp.wait_ge(y_ok, 2 * before)
                    sp.dma_start(bd[:, :], io["b_down"][bass.ds(e, 1), :].broadcast_to([P, D])).then_inc(bd_in, 16)

                load_gu(0, 0)
                with sp.Fori(0, NE // 2 - 1) as i:
                    for b in range(2):
                        load_down(2 * i + b)
                        load_gu(2 * i + b + 1, 1 - b)
                load_down(NE - 2)
                load_gu(NE - 1, 1)
                load_down(NE - 1)

            @block.tensor
            def _(pe):
                def transpose_x(g, h, slot):
                    pe.wait_ge(xg_in, 16 * g + 16)
                    for j in range(4):
                        k = 4 * h + j
                        mm = pe.transpose(bank[slot][:, j * P:(j + 1) * P], xg[:, k * P:(k + 1) * P], ident[:, :])
                    mm.then_inc(tx_mm, 1)

                def transpose_a(g, h, slot):
                    pe.wait_ge(a_ok, 2 * g + h + 1)
                    for j in range(4):
                        k = 4 * h + j
                        mm = pe.transpose(bank[slot][:, j * P:(j + 1) * P], a[:, k * P:(k + 1) * P], ident[:, :])
                    mm.then_inc(ta_mm, 1)

                def down(g, half, c, first, last):
                    for j in range(4):
                        k = 4 * half + j
                        mm = pe.matmul(bank[4 + c][:, :], aT[:, k, :], wd[:, k, c * 512:(c + 1) * 512],
                                       start=first and j == 0, stop=last and j == 3)
                    if last:
                        mm.then_inc(y_mm, 1)

                def tile(i, b, g):
                    e = 2 * i + b
                    pe.wait_ge(gu_in[b], 16 * i + 16)
                    pe.wait_ge(tx_ev, 2 * g + 2)
                    for q in range(4):
                        h, u = q // 2, q % 2
                        if q == 0:
                            pe.wait_ge(g_ev, 4 * g)
                        c0 = u * D + h * 512
                        for k in range(KT):
                            mm = pe.matmul(bank[q][:, :], xT[:, k, :], wgu[:, b, k, c0:c0 + 512],
                                           start=(k == 0), stop=(k == KT - 1))
                        mm.then_inc(gu_mm, 1)
                    transpose_a(g, 0, 6)
                    transpose_x(g + 1, 0, 7)
                    pe.wait_ge(wd_in, 16 * e + 16)
                    pe.wait_ge(ta_ev, 2 * g + 1)
                    pe.wait_ge(y_ok, 2 * g)
                    down(g, 0, 0, True, False)
                    transpose_x(g + 1, 1, 6)
                    pe.wait_ge(tx_ev, 2 * g + 3)
                    transpose_a(g, 1, 7)
                    down(g, 0, 1, True, False)
                    pe.wait_ge(ta_ev, 2 * g + 2)
                    down(g, 1, 0, False, True)
                    down(g, 1, 1, False, True)

                transpose_x(0, 0, 7)
                transpose_x(0, 1, 6)
                with pe.Fori(0, NE // 2) as i:
                    for b in range(2):
                        n, before = expert_tiles(pe, 2 * i + b)
                        with pe.Fori(0, n) as r:
                            tile(i, b, before + r)

            @block.scalar
            def _(act):
                def copy_x(g, h, slot):
                    act.wait_ge(tx_mm, 2 * g + 1 + h)
                    act.activation(xT[:, 4 * h:4 * h + 4, :].rearrange("p a b -> p (a b)"), bank[slot][:, :],
                                   ACT.Copy).then_inc(tx_ev, 1)

                def copy_a(g, h, slot):
                    act.wait_ge(ta_mm, 2 * g + 1 + h)
                    act.activation(aT[:, 4 * h:4 * h + 4, :].rearrange("p a b -> p (a b)"), bank[slot][:, :],
                                   ACT.Copy).then_inc(ta_ev, 1)

                def tile(g):
                    for h in range(2):
                        act.wait_ge(gate_ok, 2 * g + h + 1)
                        act.activation(sig[:, :], gate[:, :], ACT.Sigmoid, scale=ALPHA).then_inc(sig_ok, 1)
                    copy_a(g, 0, 6)
                    copy_x(g + 1, 0, 7)
                    copy_x(g + 1, 1, 6)
                    copy_a(g, 1, 7)

                copy_x(0, 0, 7)
                copy_x(0, 1, 6)
                with act.Fori(0, NE) as e:
                    n, before = expert_tiles(act, e)
                    with act.Fori(0, n) as r:
                        tile(before + r)

            @block.vector
            def _(dve):
                def tile(e, g):
                    ch = Chain(dve, gch, g * NG)
                    dve.wait_ge(bg_in, 16 * e + 16)
                    for h in range(2):
                        cs = slice(h * 512, (h + 1) * 512)
                        dve.wait_ge(gu_mm, 4 * g + 2 * h + 1)
                        dve.tensor_tensor(gate[:, :], bank[2 * h][:, :], bgu[:, cs], ALU.add).then_inc(g_ev, 1)
                        dve.wait_ge(g_ev, 4 * g + 2 * h + 1)
                        dve.tensor_scalar(gate[:, :], gate[:, :], LIMIT, None, ALU.min).then_inc(gate_ok, 1)
                        dve.wait_ge(gu_mm, 4 * g + 2 * h + 2)
                        dve.tensor_tensor(up[:, :], bank[2 * h + 1][:, :], bgu[:, D + h * 512:D + (h + 1) * 512],
                                          ALU.add).then_inc(g_ev, 1)
                        dve.wait_ge(g_ev, 4 * g + 2 * h + 2)
                        ch.link(dve.tensor_scalar(up[:, :], up[:, :], -LIMIT, LIMIT, ALU.max, ALU.min))
                        dve.wait_ge(sig_ok, 2 * g + h + 1)
                        ch.link(dve.tensor_tensor(gate[:, :], gate[:, :], sig[:, :], ALU.mult))
                        dve.wait_ge(ta_mm, 2 * g + h)
                        dve.scalar_tensor_tensor(a[:, cs], up[:, :], 1.0, gate[:, :], ALU.add,
                                                 ALU.mult).then_inc(a_ok, 1)
                        dve.wait_ge(a_ok, 2 * g + h + 1)
                    dve.wait_ge(bd_in, 16 * e + 16)
                    dve.wait_ge(idc_ok, g + 1)
                    dve.wait_ge(sc, 16 * g + 16)
                    for c in range(2):
                        cs = slice(c * 512, (c + 1) * 512)
                        dve.wait_ge(y_mm, 2 * g + c + 1)
                        ch.link(dve.tensor_tensor(y[:, cs], bank[4 + c][:, :], bd[:, cs], ALU.add))
                        dve.scalar_tensor_tensor(y[:, cs], y[:, cs], idc[:, 1:2], gtf[:, cs], ALU.mult,
                                                 ALU.mult).then_inc(y_ok, 1)
                    assert ch.n == NG
                dve.wait_ge(cin, 32)
                dve.memset(y[:, :], 0.0).then_inc(go, 1)
                with dve.Fori(0, NE) as e:
                    n, before = expert_tiles(dve, e)
                    with dve.Fori(0, n) as r:
                        tile(e, before + r)

            @block.gpsimd
            def _(pool):
                pool.wait_ge(cin, 32)
                pool.memset(idc[:, :], 0.0).then_inc(pch, 1)
                pool.wait_ge(pch, 1)
                pool.tensor_scalar(idc[:, 0:1].bitcast(I32), pidx[:, 0:1], float(SEQ), None, ALU.add).then_inc(pch, 1)
                hold(pool, go, (pch, 2))

                def scatter():
                    pool.indirect_dma_start(acc_d, bass.IndirectOffsetOnAxis(ap=idc[:, 0:1].bitcast(I32), axis=0),
                                            y[:, :], None, compute_op=ALU.add).then_inc(sc, 16)

                def gather():
                    pool.indirect_dma_start(xg[:, :], None, h2_d, bass.IndirectOffsetOnAxis(
                        ap=idn[:, 0:1].bitcast(I32), axis=0)).then_inc(xg_in, 16)

                def tile(e, r, g):
                    pool.dma_start(idn[:, :], list_d[bass.ds(e * CAP + r * P, P), :]).then_inc(li, 16)
                    hold(pool, go, (li, 16 * g + 16), (tx_mm, 2 * g))
                    gather()
                    hold(pool, go, (y_ok, 2 * g))
                    scatter()
                    hold(pool, go, (sc, 16 * g + 16), (xg_in, 16 * g + 16))
                    pool.tensor_copy(idc[:, :], idn[:, :]).then_inc(idc_ok, 1)
                    hold(pool, go, (idc_ok, g + 1))

                with pool.Fori(0, NE) as e:
                    n, before = expert_tiles(pool, e)
                    with pool.Fori(0, n) as r:
                        tile(e, r, before + r)
                total = pool.value_load(table[0:1, 2 * NE:2 * NE + 1], min_val=NE, max_val=TOPK * NT + NE)
                hold(pool, go, (tx_mm, 2 * total))
                gather()
                hold(pool, go, (y_ok, 2 * total))
                scatter()
                hold(pool, go, (sc, 16 * total + 16), (xg_in, 16 * total + 16))
                pool.sem_inc(go, 1)


def stage5(nc, io, sb, sem, acc_d):
    R = 4
    with ExitStack() as ctx:
        xf = sb(ctx, "xf", [P, R, D])
        yf = sb(ctx, "yf", [P, R, D])
        sq = sb(ctx, "sq5", [P, D])
        st = sb(ctx, "st5", [P, R])
        rs = sb(ctx, "rs5", [P, R])
        ms = sb(ctx, "ms5", [P, R])
        rt = sb(ctx, "rt5", [P, R])
        gf = sb(ctx, "gf", [P, D])
        cin, ss_ok, f_ok, vch, ms_ok, rt_ok = (sem(f"s5_{n}") for n in (
            "gain_in", "squares_summed", "result_ready", "vector_chain", "mean_square", "root"))
        x_in, f_out = ([sem(f"s5_{n}{i}") for i in range(R)] for n in ("rows_in", "result_stored"))
        with nc.Block() as block:
            @block.sync
            def _(sp):
                sp.dma_start(gf[:, :], io["g_final"].broadcast_to([P, D])).then_inc(cin, 16)
                with sp.Fori(0, NT // R) as i:
                    for j in range(R):
                        sp.wait_ge(f_ok, R * i)
                        sp.dma_start(xf[:, j, :], acc_d[bass.ds((i * R + j) * P, P), :]).then_inc(x_in[j], 16)

            @block.scalar
            def _(act):
                with act.Fori(0, NT // R) as i:
                    for j in range(R):
                        act.wait_ge(x_in[j], 16 * i + 16)
                        act.wait_ge(f_ok, R * i)
                        act.activation(sq[:, :], xf[:, j, :], ACT.Square, accum_out=st[:, j:j + 1]).then_inc(ss_ok, 1)
                        act.wait_ge(ms_ok, i * R + j + 1)
                        act.activation(rt[:, j:j + 1], ms[:, j:j + 1], ACT.Sqrt).then_inc(rt_ok, 1)

            @block.vector
            def _(dve):
                dve.wait_ge(cin, 16)
                with dve.Fori(0, NT // R) as i:
                    ch = Chain(dve, vch, R * i)
                    for j in range(R):
                        dve.wait_ge(ss_ok, i * R + j + 1)
                        dve.tensor_scalar(ms[:, j:j + 1], st[:, j:j + 1], 1.0 / D, EPS, ALU.mult,
                                          ALU.add).then_inc(ms_ok, 1)
                        dve.wait_ge(rt_ok, i * R + j + 1)
                        ch.link(dve.reciprocal(rs[:, j:j + 1], rt[:, j:j + 1]))
                        dve.wait_ge(f_out[j], 16 * i)
                        dve.scalar_tensor_tensor(yf[:, j, :], xf[:, j, :], rs[:, j:j + 1], gf[:, :], ALU.mult,
                                                 ALU.mult).then_inc(f_ok, 1)

            @block.gpsimd
            def _(pool):
                with pool.Fori(0, NT // R) as i:
                    for j in range(R):
                        pool.wait_ge(f_ok, i * R + j + 1)
                        pool.wait_ge(cin, 16)
                        pool.dma_start(io["out"][bass.ds((i * R + j) * P, P), :], yf[:, j, :]).then_inc(f_out[j], 16)
                for j in range(R):
                    pool.wait_ge(f_out[j], 16 * NT // R)


def shape_constants():
    rot = np.zeros((P, P), np.float32)
    freq = np.zeros((P, 1), np.float32)
    theta = np.float32(500000.0) ** (-np.arange(0, 2 * ROPE_HALF, 2, dtype=np.float32) / np.float32(2 * ROPE_HALF))
    for base in (0, HD):
        for f in range(ROPE_HALF):
            lo, hi = base + f, base + ROPE_HALF + f
            rot[hi, lo] = -1.0
            rot[lo, hi] = 1.0
            freq[lo, 0] = freq[hi, 0] = theta[f]
    return {
        "ident": np.eye(P, dtype=np.float32), "rot": rot, "freq": freq,
        "tri": np.triu(np.ones((P, P), np.float32), 1),
        "iota_e": np.arange(NE, dtype=np.float32)[None, :],
        "expert_offset": (np.arange(NE, dtype=np.float32) * CAP)[None, :],
        "partition_index": np.arange(P, dtype=np.float32)[:, None],
    }


def kernel(**inputs):
    import concourse.bacc as _bacc
    from concourse.bass_utils import run_bass_kernel_spmd as _run

    g = {k: np.asarray(v) for k, v in inputs.items()}
    arrays = {
        "x": g["x"][0],
        "c_col": np.ascontiguousarray(g["c"].reshape(KT, P).T),
        "g_mix_col": np.ascontiguousarray(g["g_mix_norm"].reshape(KT, P).T),
        "positions": g["positions"],
        "w_ada": g["w_ada"][0], "b_ada": g["b_ada"],
        "w_in": g["w_in"][0],
        "rel_rev": np.ascontiguousarray(g["rel_bias"][0, :, ::-1]),
        "lambdas": np.concatenate([g["lambda_q1"], g["lambda_k1"], g["lambda_q2"], g["lambda_k2"]]),
        "g_subln": g["g_subln"],
        "w_out": g["w_out"][0],
        "g_ffn_norm": g["g_ffn_norm"],
        "w_router": g["w_router"][0], "b_router": g["b_router"],
        "w_gate_up": g["w_gate_up"][0], "b_gate_up": g["b_gate_up"][0],
        "w_down": g["w_down"][0], "b_down": g["b_down"][0],
        "g_final": g["g_final"][None, :],
        **shape_constants(),
    }
    nc = _bacc.Bacc("TRN2", target_bir_lowering=False, num_devices=1)
    io = {n: nc.dram_tensor(f"in_{n}", a.shape, mybir.dt.from_np(a.dtype), kind="ExternalInput").ap()
          for n, a in arrays.items()}
    for n, shape in (("mod_scratch", (1, NMOD * D)), ("o_scratch", (SEQ, D)), ("acc_scratch", (ROWS, D)),
                     ("h2_scratch", (ROWS, D)), ("list_scratch", (NE * CAP, 2)), ("toe_scratch", (A_HEADS, TOE)),
                     ("bias_scratch", (A_HEADS, P, TOE))):
        io[n] = nc.dram_tensor(n, shape, F32, kind="Internal").ap()
    io["out"] = nc.dram_tensor("out_0", (SEQ, D), F32, kind="ExternalOutput").ap()
    build_program(nc, io)
    r = _run(nc, [{f"in_{n}": a for n, a in arrays.items()}], core_ids=[0])
    return r.results[0]["out_0"].reshape(1, SEQ, D)
```

```python
from contextlib import ExitStack

import numpy as np

import concourse.bass as bass
from concourse import mybir

P = 128
D = 1024
KT = D // P
SEQ = 2048
NT = SEQ // P
NG4 = SEQ // 512
NMOD = 6
HD = 64
A_HEADS = 8
B_HEADS = 4
AW = A_HEADS * HD
BW = B_HEADS * 2 * HD
IN_W = 3 * AW + 2 * BW + BW
UNITS = 4
BAND_T = 5
BAND = BAND_T * P
MAX_REL = 128
RELW = 2 * MAX_REL + 1
TOE = BAND + P - 1
NE = 32
TOPK = 4
TOK = 320
SMALL = 256
CAP = -(-SEQ // TOK) * TOK + TOK
PADS = CAP * NE // P
ROWS = SEQ + PADS
ALPHA = 1.702
LIMIT = 7.0
EPS = 1e-6
NEG = -1e30
LAM0 = 0.8 - 0.6
ROPE_HALF = 8
SCALE = HD ** -0.5
SHIFT = 8.0

F32 = mybir.dt.float32
F32R = mybir.dt.float32r
I32 = mybir.dt.int32
U32 = mybir.dt.uint32
ALU = mybir.AluOpType
ACT = mybir.ActivationFunctionType
AX = mybir.AxisListType.X


class Chain:

    def __init__(self, eng, sem, base=0):
        self.eng, self.sem, self.base, self.n = eng, sem, base, 0

    def add(self, ins):
        ins.then_inc(self.sem, 1)
        self.n += 1
        return self.base + self.n

    def link(self, ins):
        self.add(ins)
        self.eng.wait_ge(self.sem, self.base + self.n)


def hold(eng, started, *waits):
    values = [(s, v if isinstance(v, int) else eng.to_reg(v)) for s, v in waits]
    eng.wait_ge(started, 1)
    for s, v in values:
        eng.wait_ge(s, v)


def build_program(nc, io):
    with ExitStack() as top:
        persistent = top

        def sb(ctx, name, shape, dt=F32):
            return ctx.enter_context(nc.sbuf_tensor(name, shape, dt))

        taken = []

        def sem(name):
            taken.append(nc.alloc_semaphore(name=name))
            return taken[-1]

        bank = [top.enter_context(nc.psum_tensor(f"bank{i}", [P, 512], F32)) for i in range(8)]
        ident = sb(persistent, "ident", [P, P])
        loaded = sem("constants_loaded")
        mod_d, o_d, acc_d, h2_d, list_d, toe_d = (
            io["mod_scratch"], io["o_scratch"], io["acc_scratch"], io["h2_scratch"],
            io["list_scratch"], io["toe_scratch"])

        stage1_and_2(nc, io, top, sb, sem, bank, ident, loaded, mod_d, o_d, toe_d)
        nc.clear_and_free_semaphores(taken)
        nc.all_engine_barrier()
        table = sb(persistent, "tile_table", [1, 5 * NE], I32)
        stage3(nc, io, sb, sem, bank, ident, mod_d, o_d, acc_d, h2_d, list_d, table)
        stage4(nc, io, sb, sem, bank, ident, mod_d, acc_d, h2_d, list_d, table)
        stage5(nc, io, sb, sem, acc_d)


def stage1_and_2(nc, io, top, sb, sem, bank, ident, loaded, mod_d, o_d, toe_d):
    with ExitStack() as ctx:
        hT = sb(ctx, "hT", [P, KT, SEQ])
        cosT = sb(ctx, "cosT", [P, SEQ])
        sinT = sb(ctx, "sinT", [P, SEQ])
        rot = sb(ctx, "rot", [P, P])
        stage1(nc, io, sb, sem, bank, ident, loaded, mod_d, toe_d, hT, cosT, sinT, rot)
        stage2(nc, io, sb, sem, bank, ident, o_d, toe_d, hT, cosT, sinT, rot)


def stage1(nc, io, sb, sem, bank, ident, loaded, mod_d, toe_d, hT, cosT, sinT, rot):
    NCH = NMOD * D // 512
    with ExitStack() as ctx:
        ccol = sb(ctx, "ccol", [P, KT])
        csig = sb(ctx, "csig", [P, KT])
        cact = sb(ctx, "cact", [P, KT])
        gmix = sb(ctx, "gmix", [P, KT])
        one = sb(ctx, "one", [1, 1])
        wada = sb(ctx, "wada", [P, 2, KT, 512])
        bada = sb(ctx, "bada", [1, 2, 512])
        mrow = sb(ctx, "mrow", [1, 2, 512])
        mcol = sb(ctx, "mcol", [P, 2 * KT])
        gcol = sb(ctx, "gcol", [P, KT])
        xt = sb(ctx, "xt", [P, 4, D])
        xsq = sb(ctx, "xsq", [P, D])
        xss = sb(ctx, "xss", [P, 4])
        xrs = sb(ctx, "xrs", [P, 4])
        xms = sb(ctx, "xms", [P, 4])
        xrt = sb(ctx, "xrt", [P, 4])
        posi = sb(ctx, "posi", [P, SEQ], I32)
        ang = sb(ctx, "ang", [P, SEQ])
        kk = sb(ctx, "kk", [P, SEQ])
        kh = sb(ctx, "kh", [P, SEQ])
        freq = sb(ctx, "freq", [P, 1])
        relr = sb(ctx, "relr", [A_HEADS, RELW])
        toe = sb(ctx, "toe", [A_HEADS, TOE])

        w_in = [sem(f"ada_loaded{i}") for i in range(2)]
        b_in = [sem(f"ada_bias_loaded{i}") for i in range(2)]
        m_mm = sem("mod_product")
        m_add = sem("mod_added")
        m_out = [sem(f"mod_stored{i}") for i in range(2)]
        c_rdy = sem("c_activated")
        csg = sem("c_sigmoid")
        mc_mm = sem("mod_columns_product")
        mc_ok = sem("mod_columns_ready")
        x_in = sem("x_loaded")
        ss_ok = sem("x_squares_summed")
        xn_ok = sem("x_normalised")
        ms_ok = sem("x_mean_square")
        rt_ok = sem("x_root")
        xt_mm = sem("x_transposed")
        h_ok = sem("h_columns_written")
        vch = sem("stage1_vector_chain")
        angs = sem("angles_reduced")
        abss = sem("cos_argument_ready")
        trig = sem("tables_written")
        toes = sem("toeplitz_built")
        pch = sem("stage1_pool_chain")
        toe_out = sem("toeplitz_stored")
        bias_out = sem("bias_tiles_stored")

        with nc.Block() as block:
            @block.sync
            def _(sp):
                sp.dma_start(ccol[:, :], io["c_col"]).then_inc(loaded, 16)
                sp.dma_start(gmix[:, :], io["g_mix_col"]).then_inc(loaded, 16)
                sp.dma_start(ident[:, :], io["ident"]).then_inc(loaded, 16)
                sp.dma_start(rot[:, :], io["rot"]).then_inc(loaded, 16)
                sp.dma_start(freq[:, :], io["freq"]).then_inc(loaded, 16)
                sp.dma_start(posi[:, :], io["positions"].broadcast_to([P, SEQ])).then_inc(loaded, 16)
                sp.dma_start(relr[:, :], io["rel_rev"]).then_inc(loaded, 16)
                for n in range(NCH):
                    if n >= 2:
                        sp.wait_ge(m_mm, n - 1)
                    sp.dma_start(wada[:, n % 2], io["w_ada"][:, n * 512:(n + 1) * 512]
                                 .rearrange("(k p) n -> p k n", p=P)).then_inc(w_in[n % 2], 16)
                    if n >= 2:
                        sp.wait_ge(m_add, n - 1)
                    sp.dma_start(bada[:, n % 2, :], io["b_ada"][:, n * 512:(n + 1) * 512]).then_inc(b_in[n % 2], 16)
                sp.wait_ge(toe_out, 16)
                for h in range(A_HEADS):
                    sp.dma_start(io["bias_scratch"][h], toe_d[h:h + 1, :].broadcast_to([P, TOE])).then_inc(bias_out, 16)
                sp.wait_ge(bias_out, 16 * A_HEADS)

            @block.tensor
            def _(pe):
                pe.wait_ge(c_rdy, 1)
                for n in range(NCH):
                    pe.wait_ge(w_in[n % 2], 16 * (n // 2 + 1))
                    if n >= 2:
                        pe.wait_ge(m_add, n - 1)
                    for k in range(KT):
                        mm = pe.matmul(bank[n % 2][0:1, :], cact[:, k:k + 1], wada[:, n % 2, k, :],
                                       start=(k == 0), stop=(k == KT - 1))
                    mm.then_inc(m_mm, 1)
                    if n < 4:
                        pe.wait_ge(m_add, n + 1)
                        for j in range(4):
                            mm = pe.matmul(bank[2][:, 4 * n + j:4 * n + j + 1],
                                           mrow[0:1, n % 2, j * P:(j + 1) * P], one[0:1, 0:1],
                                           start=True, stop=True)
                        mm.then_inc(mc_mm, 1)
                for g in range(NG4):
                    pe.wait_ge(xn_ok, 4 * (g + 1))
                    for k in range(KT):
                        n = g * KT + k
                        if n >= 4:
                            pe.wait_ge(h_ok, n - 3)
                        for j in range(4):
                            mm = pe.transpose(bank[4 + n % 4][:, j * P:(j + 1) * P],
                                              xt[:, j, k * P:(k + 1) * P], ident[:, :])
                        mm.then_inc(xt_mm, 1)

            @block.scalar
            def _(act):
                act.wait_ge(loaded, 16 * 7)
                act.activation(csig[:, :], ccol[:, :], ACT.Sigmoid).then_inc(csg, 1)
                for g in range(NG4):
                    if g >= 1:
                        act.wait_ge(xt_mm, KT * g)
                    for j in range(4):
                        t = 4 * g + j
                        act.dma_start(xt[:, j, :], io["x"][t * P:(t + 1) * P, :]).then_inc(x_in, 16)
                    act.wait_ge(x_in, 64 * (g + 1))
                    for j in range(4):
                        t = 4 * g + j
                        if t >= 1:
                            act.wait_ge(ss_ok, t)
                        act.activation(xsq[:, :], xt[:, j, :], ACT.Square,
                                       accum_out=xss[:, j:j + 1]).then_inc(ss_ok, 1)
                    act.wait_ge(ms_ok, g + 1)
                    act.activation(xrt[:, :], xms[:, :], ACT.Sqrt).then_inc(rt_ok, 1)
                    if g == 0:
                        act.wait_ge(angs, 1)
                        act.activation(sinT[:, :], ang[:, :], ACT.Sin).then_inc(trig, 1)
                        act.wait_ge(abss, 1)
                        act.activation(cosT[:, :], kk[:, :], ACT.Sin).then_inc(trig, 1)

            @block.vector
            def _(dve):
                ch = Chain(dve, vch)
                ch.link(dve.memset(one[:, :], 1.0))
                dve.wait_ge(loaded, 16 * 7)
                dve.wait_ge(csg, 1)
                dve.tensor_tensor(cact[:, :], ccol[:, :], csig[:, :], ALU.mult).then_inc(c_rdy, 1)
                two_pi = 2.0 * np.pi
                parts, rest = [], two_pi
                for bits in (2 ** 9, 2 ** 21, 2 ** 33):
                    part = float(np.floor(rest * bits) / bits)
                    parts.append(part)
                    rest -= part
                parts.append(rest)
                magic = 1.5 * 2.0 ** 23
                big = magic * 4096.0
                ch.link(dve.tensor_copy(ang[:, :], posi[:, :]))
                ch.link(dve.tensor_scalar(ang[:, :], ang[:, :], freq[:, 0:1], None, ALU.mult))
                ch.link(dve.tensor_scalar(kk[:, :], ang[:, :], 1.0 / two_pi, None, ALU.mult))
                ch.link(dve.tensor_scalar(kk[:, :], kk[:, :], magic, None, ALU.add))
                ch.link(dve.tensor_scalar(kk[:, :], kk[:, :], -magic, None, ALU.add))
                ch.link(dve.tensor_scalar(kh[:, :], kk[:, :], big, None, ALU.add))
                ch.link(dve.tensor_scalar(kh[:, :], kh[:, :], -big, None, ALU.add))
                ch.link(dve.tensor_tensor(kk[:, :], kk[:, :], kh[:, :], ALU.subtract))
                for part in parts:
                    for m in (kh, kk):
                        ch.link(dve.scalar_tensor_tensor(ang[:, :], m[:, :], -part, ang[:, :],
                                                         ALU.mult, ALU.add))
                ch.link(dve.tensor_scalar(ang[:, :], ang[:, :], float(np.float32(3.1415925)),
                                          float(np.float32(-3.1415925)), ALU.min, ALU.max))
                dve.sem_inc(angs, 1)
                ch.link(dve.scalar_tensor_tensor(kk[:, :], ang[:, :], -1.0, ang[:, :], ALU.mult, ALU.max))
                dve.tensor_scalar(kk[:, :], kk[:, :], -1.0, float(np.pi / 2), ALU.mult, ALU.add).then_inc(abss, 1)
                for n in range(NCH):
                    dve.wait_ge(m_mm, n + 1)
                    dve.wait_ge(b_in[n % 2], 16 * (n // 2 + 1))
                    if n >= 2:
                        dve.wait_ge(m_out[n % 2], 16 * (n // 2))
                        dve.wait_ge(mc_mm, min(n - 1, 4))
                    dve.tensor_tensor(mrow[:, n % 2, :], bank[n % 2][0:1, :], bada[:, n % 2, :],
                                      ALU.add).then_inc(m_add, 1)
                    if n == 3:
                        dve.wait_ge(mc_mm, 4)
                        ch.link(dve.tensor_copy(mcol[:, :], bank[2][:, 0:2 * KT]))
                        ch.link(dve.tensor_scalar(gcol[:, :], mcol[:, KT:2 * KT], 1.0, None, ALU.add))
                        ch.link(dve.tensor_tensor(gcol[:, :], gcol[:, :], gmix[:, :], ALU.mult))
                for g in range(NG4):
                    dve.wait_ge(ss_ok, 4 * (g + 1))
                    dve.tensor_scalar(xms[:, :], xss[:, :], 1.0 / D, EPS, ALU.mult, ALU.add).then_inc(ms_ok, 1)
                    dve.wait_ge(rt_ok, g + 1)
                    ch.link(dve.reciprocal(xrs[:, :], xrt[:, :]))
                    for j in range(4):
                        dve.tensor_scalar(xt[:, j, :], xt[:, j, :], xrs[:, j:j + 1], None,
                                          ALU.mult).then_inc(xn_ok, 1)
                    for k in range(KT):
                        n = g * KT + k
                        dve.wait_ge(xt_mm, n + 1)
                        dve.tensor_scalar(hT[:, k, g * 512:(g + 1) * 512], bank[4 + n % 4][:, :],
                                          gcol[:, k:k + 1], mcol[:, k:k + 1], ALU.mult,
                                          ALU.add).then_inc(h_ok, 1)

            @block.gpsimd
            def _(pool):
                ch = Chain(pool, pch)
                pool.wait_ge(loaded, 16 * 7)
                ch.link(pool.memset(toe[:, :], 0.0))
                ch.link(pool.tensor_scalar(toe[:, 0:512], toe[:, 0:512], relr[:, 0:1], None, ALU.add))
                ch.link(pool.tensor_copy(toe[:, 511:TOE], relr[:, 0:256]))
                ch.link(pool.tensor_scalar(toe[:, :], toe[:, :], 1.0 / SCALE, None, ALU.mult))
                pool.dma_start(toe_d, toe[:, :]).then_inc(toe_out, 16)
                for n in range(NCH):
                    pool.wait_ge(m_add, n + 1)
                    pool.dma_start(mod_d[:, n * 512:(n + 1) * 512], mrow[:, n % 2, :]).then_inc(m_out[n % 2], 16)
                for m in m_out:
                    pool.wait_ge(m, 16 * NCH // 2)
                pool.wait_ge(toe_out, 16)
                pool.wait_ge(trig, 2)


def score_plan(group):
    plan = []
    for t in range(NT):
        k0 = max(0, t - (BAND_T - 1)) if group == "A" else 0
        n = t - k0 + 1
        sizes = [4] * (n // 4) + ([n % 4] if n % 4 else [])
        if n > 4 and sizes[-1] == 1:
            sizes[-2:] = [3, 2]
        pieces = [(k0 + sum(sizes[:i]), m) for i, m in enumerate(sizes)]
        values = pieces
        plan.append((k0, n, pieces, values))
    return plan


def stage2(nc, io, sb, sem, bank, ident, o_d, toe_d, hT, cosT, sinT, rot):
    with ExitStack() as ctx:
        wq = sb(ctx, "wq", [P, KT, P])
        wk = sb(ctx, "wk", [P, KT, P])
        v_all = sb(ctx, "v_all", [P, NT, 512])
        q2 = [sb(ctx, f"q2_{c}", [P, SEQ], F32R) for c in range(2)]
        k_hi = [sb(ctx, f"k_hi{c}", [P, SEQ], F32R) for c in range(2)]
        k_lo = [sb(ctx, f"k_lo{c}", [P, SEQ], F32R) for c in range(2)]
        S0 = sb(ctx, "S0", [P, 2, SEQ])
        S1 = sb(ctx, "S1", [P, SEQ])
        PT = sb(ctx, "PT", [P, 4, 512])
        bias = sb(ctx, "bias", [P, 2, BAND])
        osb = sb(ctx, "osb", [P, 2, P])
        pm = sb(ctx, "pm", [P, 2, 2, 4])
        nm = sb(ctx, "nm", [P, 2, 2])
        l = sb(ctx, "l", [P, 2, 2])
        r = sb(ctx, "r", [P, 2, 2])
        lams = sb(ctx, "lams", [P, 4])
        wv = [S0[:, h, :].rearrange("p (k n) -> p k n", k=KT) for h in range(2)]
        lamv = PT[:, 0, 0:4 * HD].rearrange("p (a d) -> p a d", a=4)
        lamt = PT[:, 1, 0:HD]
        mask = bias[:, 0, :]
        sbank, tbank, obank = bank[0:4], bank[4:6], bank[6:8]
        go = sem("stage2_go")
        sconst = sem("stage2_constants")
        lamch, lam_dots, lam_exp = sem("lambda_chain"), sem("lambda_dots"), sem("lambda_exponentials")

        for group in ("A", "B"):
            A = group == "A"
            plan = score_plan(group)
            NPC = 2 * sum(len(p[2]) for p in plan)
            NVC = (2 if A else 1) * sum(len(p[3]) for p in plan)
            NEV = NVC // 2
            assert NVC % 4 == 0
            q0 = 0 if A else 3 * AW
            k0c = AW if A else 3 * AW + BW
            v0 = 2 * AW if A else 3 * AW + 2 * BW
            s = {n: sem(f"{n}_{group}") for n in (
                "wv_in", "v_mm", "v_ev", "wqk_in", "proj_mm", "proj_ev", "rot_mm", "rot_ok", "bias_in",
                "score_mm", "score_ev", "max_ok", "exp_ok", "val_tr", "ev_act", "ev_dve", "pv_mm",
                "o_ev", "o_out0", "o_out1", "wv_in1", "hi_ok", "lo_ok", "ratio_ok", "comb_ok", "dch", "mask_ok", "rope_done")}
            pc0, vc0 = [0], [0]
            for p in plan:
                pc0.append(pc0[-1] + 2 * len(p[2]))
                vc0.append(vc0[-1] + (2 if A else 1) * len(p[3]))
            OC = 0 if A else AW
            OE = 2 if A else 1

            def val_pieces(t):
                out, i = [], vc0[t]
                for h in range(2 if A else 1):
                    vs = plan[t][3]
                    for j, (kt, n) in enumerate(vs):
                        out.append((i, h, kt, n, j == 0, j == len(vs) - 1))
                        i += 1
                return out

            def scores(b, c):
                if c == 0:
                    return S0[:, b, :]
                return S1[:, b * (SEQ // 2):(b + 1) * (SEQ // 2)] if A else S1[:, :]

            def parts_before(n):
                return 2 * n if n <= 4 else 8 + 4 * (n - 4)

            def parts(n):
                for c in range(2):
                    own, other = slice(c * HD, (c + 1) * HD), slice((1 - c) * HD, (2 - c) * HD)
                    if n < 4:
                        yield q2[c], q2[c], own, own, other
                    else:
                        yield k_hi[c], k_lo[c], own, own, own
                        yield k_hi[c], k_lo[c], own, other, other

            def rotate(pe, u, n):
                pe.wait_ge(s["proj_ev"], 8 * u + n + 1)
                if n >= 2:
                    pe.wait_ge(s["rot_ok"], 8 * u + n - 1)
                else:
                    pe.wait_ge(s["o_ev"], OE * u * NT)
                pe.matmul(obank[n % 2][:, :], rot[:, :], PT[:, n % 2, :],
                          start=True, stop=True).then_inc(s["rot_mm"], 1)

            def values(pe, u, t):
                ps = val_pieces(t)

                def tr(p):
                    i, h, kt, n, first, last = p
                    kk0 = plan[t][0]
                    if A:
                        pe.wait_ge(s["exp_ok"], u * 2 * NT + 2 * t + h + 1)
                    else:
                        pe.wait_ge(s["comb_ok"], u * NVC + i + 1)
                    if i >= 2:
                        pe.wait_ge(s["ev_dve"] if i % 2 else s["ev_act"], u * NEV + i // 2)
                    for j in range(n):
                        b = kt - kk0 + j
                        mm = pe.transpose(tbank[i % 2][:, j * P:(j + 1) * P],
                                          scores(t % 2, h)[:, b * P:(b + 1) * P], ident[:, :])
                    mm.then_inc(s["val_tr"], 1)

                def pv(p):
                    i, h, kt, n, first, last = p
                    pe.wait_ge(s["ev_dve"] if i % 2 else s["ev_act"], u * NEV + i // 2 + 1)
                    if first and h == 0:
                        pe.wait_ge(s["o_ev"], OE * (u * NT + max(0, t - 1)))
                    for j in range(n):
                        mm = pe.matmul(obank[t % 2][:, h * P:(h + 1) * P], PT[:, i % 4, j * P:(j + 1) * P],
                                       v_all[:, kt + j, bass.ds(u * P, P)],
                                       start=(first and j == 0), stop=(last and j == n - 1))
                    mm.then_inc(s["pv_mm"], 1)

                for j, p in enumerate(ps):
                    tr(p)
                    if j:
                        pv(ps[j - 1])
                pv(ps[-1])

            def evacuate(eng, done, u, i, n):
                if i >= 4:
                    eng.wait_ge(s["pv_mm"], u * NVC + i - 3)
                eng.wait_ge(s["val_tr"], u * NVC + i + 1)
                src, dst = tbank[i % 2][:, 0:n * P], PT[:, i % 4, 0:n * P]
                if i % 2:
                    eng.tensor_copy(dst, src).then_inc(done, 1)
                else:
                    eng.activation(dst, src, ACT.Copy).then_inc(done, 1)

            def output(dve, u, t, ch):
                b = t % 2
                dve.wait_ge(s["pv_mm"], u * NVC + vc0[t + 1])
                out_slot_free(dve, u, t)
                if A:
                    for h in range(2):
                        dve.tensor_scalar(osb[:, t % 2, h * HD:(h + 1) * HD],
                                          obank[b][:, h * (P + HD):h * (P + HD) + HD], r[:, b, h:h + 1], None,
                                          ALU.mult).then_inc(s["o_ev"], 1)
                else:
                    dve.tensor_scalar(osb[:, t % 2, :], obank[b][:, 0:P], r[:, b, 0:1], None,
                                      ALU.mult).then_inc(s["o_ev"], 1)

            def out_slot_free(dve, u, t):
                dve.wait_ge(s[f"o_out{t % 2}"], 8 * NT * u + 16 * (t // 2))

            with nc.Block() as block:
                @block.sync
                def _(sp):
                    if not A:
                        sp.dma_start(lamv, io["lambdas"].rearrange("(o a) d -> o a d", o=1)
                                     .broadcast_to([P, 4, HD])).then_inc(sconst, 16)

                    def load_qk(u):
                        sp.dma_start(wq[:, :, :], io["w_in"][:, bass.ds(q0 + u * P, P)]
                                     .rearrange("(k p) n -> p k n", p=P)).then_inc(s["wqk_in"], 16)
                        sp.dma_start(wk[:, :, :], io["w_in"][:, bass.ds(k0c + u * P, P)]
                                     .rearrange("(k p) n -> p k n", p=P)).then_inc(s["wqk_in"], 16)

                    for h in range(2):
                        sp.dma_start(wv[h], io["w_in"][:, v0 + 256 * h:v0 + 256 * (h + 1)]
                                     .rearrange("(k p) n -> p k n", p=P)).then_inc(s["wv_in1" if h else "wv_in"], 16)
                        if h == 0:
                            load_qk(0)

                    def unit(u, last):
                        if A:
                            sp.wait_ge(s["score_ev"], u * NPC)
                            for h in range(2):
                                src = bass.AP(io["bias_scratch"].tensor, (2 * u + h) * (P * TOE) + P - 1,
                                              [[TOE - 1, P], [1, BAND]])
                                sp.dma_start(bias[:, h, :], src).then_inc(s["bias_in"], 16)
                        if not last:
                            sp.wait_ge(s["proj_mm"], u * 8 + 8)
                            load_qk(u + 1)
                        for t in range(NT):
                            sp.wait_ge(s["o_ev"], OE * (u * NT + t + 1))
                            sp.dma_start(o_d[t * P:(t + 1) * P, bass.ds(OC + u * P, P)],
                                         osb[:, t % 2, :]).then_inc(s[f"o_out{t % 2}"], 16)
                    with sp.Fori(0, UNITS - 1) as u:
                        unit(u, False)
                    unit(UNITS - 1, True)
                    for j in range(2):
                        sp.wait_ge(s[f"o_out{j}"], 8 * NT * UNITS)

                @block.tensor
                def _(pe):
                    for h in range(2):
                        pe.wait_ge(s["wv_in1" if h else "wv_in"], 16)
                        for t in range(NT):
                            n = h * NT + t
                            if n >= 2:
                                pe.wait_ge(s["v_ev"], n - 1)
                            for k in range(KT):
                                mm = pe.matmul(tbank[n % 2][:, 0:256], hT[:, k, t * P:(t + 1) * P],
                                               wv[h][:, k, :], start=(k == 0), stop=(k == KT - 1))
                            mm.then_inc(s["v_mm"], 1)
                    pe.wait_ge(s["v_ev"], 2 * NT)
                    with pe.Fori(0, UNITS) as u:
                        pe.wait_ge(s["wqk_in"], 32 * u + 32)
                        for n in range(8):
                            w = wq if n < 4 else wk
                            g = n % 4
                            if n >= 2:
                                pe.wait_ge(s["proj_ev"], 8 * u + n - 1)
                            for k in range(KT):
                                mm = pe.matmul(tbank[n % 2][:, :], w[:, k, :], hT[:, k, g * 512:(g + 1) * 512],
                                               start=(k == 0), stop=(k == KT - 1))
                            mm.then_inc(s["proj_mm"], 1)
                            if not A and n >= 1:
                                rotate(pe, u, n - 1)
                        if not A:
                            rotate(pe, u, 7)
                        pe.wait_ge(s["lo_ok"], 24 * (u + 1))
                        for step in range(NT + 1):
                            if step < NT:
                                i = pc0[step]
                                for c in range(2):
                                    for kt, n in plan[step][2]:
                                        if i >= 4:
                                            pe.wait_ge(s["score_ev"], u * NPC + i - 3)
                                        for part in (k_hi[c], k_lo[c]):
                                            mm = pe.matmul(sbank[i % 4][:, 0:n * P],
                                                           q2[c][:, step * P:(step + 1) * P],
                                                           part[:, kt * P:(kt + n) * P],
                                                           start=part is k_hi[c], stop=part is k_lo[c])
                                        mm.then_inc(s["score_mm"], 1)
                                        i += 1
                            if step >= 1:
                                values(pe, u, step - 1)

                @block.scalar
                def _(act):
                    if not A:
                        act.wait_ge(lam_dots, 1)
                        act.activation(lams[:, 0:2], lams[:, 0:2], ACT.Exp).then_inc(lam_exp, 1)
                    for n in range(2 * NT):
                        h, t = n // NT, n % NT
                        act.wait_ge(s["v_mm"], n + 1)
                        act.activation(v_all[:, t, 256 * h:256 * (h + 1)], tbank[n % 2][:, 0:256],
                                       ACT.Copy).then_inc(s["v_ev"], 1)
                    with act.Fori(0, UNITS) as u:
                        for n in range(9):
                            if n < 8:
                                if n >= 2:
                                    act.wait_ge(s["lo_ok"], 24 * u + parts_before(n - 1))
                                act.wait_ge(s["proj_mm"], 8 * u + n + 1)
                                act.activation(PT[:, n % 2, :], tbank[n % 2][:, :], ACT.Copy).then_inc(s["proj_ev"], 1)
                            if n >= 1:
                                m = n - 1
                                cols = slice(m % 4 * 512, (m % 4 + 1) * 512)
                                act.wait_ge(s["proj_ev" if A else "rope_done"], 8 * u + m + 1)
                                for hi, lo, src, to, _to in parts(m):
                                    act.activation(hi[to, cols], PT[src, m % 2, :], ACT.Copy).then_inc(s["hi_ok"], 1)
                        def exponentials(step):
                            if step < NT:
                                n = plan[step][1] * P
                                for c in range(2):
                                    act.wait_ge(s["max_ok"], u * 2 * NT + 2 * step + c + 1)
                                    act.activation(scores(step % 2, c)[:, 0:n], scores(step % 2, c)[:, 0:n], ACT.Exp,
                                                   bias=nm[:, step % 2, c:c + 1],
                                                   accum_out=l[:, step % 2, c:c + 1]).then_inc(s["exp_ok"], 1)

                        for step in range(NT + 1):
                            if step >= 1:
                                for i, h, kt, n, first, last in val_pieces(step - 1):
                                    if i % 2 == 0:
                                        evacuate(act, s["ev_act"], u, i, n)
                            exponentials(step)

                @block.gpsimd
                def _(pool):
                    if A:
                        pool.sem_inc(go, 1)
                        with pool.Fori(0, UNITS) as u:
                            hold(pool, go, (s["bias_in"], 32 * u + 32))
                            pool.memset(bias[0:HD, :, BAND - HD:BAND], NEG * 8).then_inc(s["mask_ok"], 1)
                            pool.memset(bias[HD:P, :, 0:HD], NEG * 8).then_inc(s["mask_ok"], 1)
                    else:
                        pool.memset(mask, 0.0).then_inc(s["mask_ok"], 1)
                        pool.wait_ge(s["mask_ok"], 1)
                        pool.memset(mask[0:HD, BAND - HD:BAND], NEG * 8).then_inc(s["mask_ok"], 1)

                @block.vector
                def _(dve):
                    if not A:
                        ch = Chain(dve, lamch)
                        dve.wait_ge(sconst, 16)
                        ch.link(dve.tensor_tensor_reduce(lamt, lamv[:, 0, :], lamv[:, 1, :], 1.0, 0.0,
                                                         ALU.mult, ALU.add, lams[:, 0:1]))
                        ch.link(dve.tensor_tensor_reduce(lamt, lamv[:, 2, :], lamv[:, 3, :], 1.0, 0.0,
                                                         ALU.mult, ALU.add, lams[:, 1:2]))
                        dve.sem_inc(lam_dots, 1)
                        dve.wait_ge(lam_exp, 1)
                        ch.link(dve.tensor_tensor(lams[:, 2:3], lams[:, 1:2], lams[:, 0:1], ALU.subtract))
                        ch.link(dve.tensor_scalar(lams[:, 2:3], lams[:, 2:3], -LAM0, None, ALU.add))
                        dve.wait_ge(s["mask_ok"], 2)
                    PER = NT if A else 2 * NT + 8
                    with dve.Fori(0, UNITS) as u:
                        ch = Chain(dve, s["dch"], u * PER)
                        for n in range(8):
                            cols = slice(n % 4 * 512, (n % 4 + 1) * 512)
                            raw, tmp = PT[:, n % 2, :], PT[:, 2 + n % 2, :]
                            if not A:
                                dve.wait_ge(s["rot_mm"], 8 * u + n + 1)
                                dve.tensor_tensor(tmp, obank[n % 2][:, :], sinT[:, cols], ALU.mult).then_inc(s["rot_ok"], 1)
                                ch.link(dve.tensor_tensor(raw, raw, cosT[:, cols], ALU.mult))
                                dve.wait_ge(s["rot_ok"], 8 * u + n + 1)
                                dve.tensor_tensor(raw, raw, tmp, ALU.add).then_inc(s["rope_done"], 1)
                            dve.wait_ge(s["hi_ok"], 24 * u + parts_before(n + 1))
                            for hi, lo, src, _to, to in parts(n):
                                dve.tensor_tensor(lo[to, cols], PT[src, n % 2, :], hi[src, cols].bitcast(F32),
                                                  ALU.subtract).then_inc(s["lo_ok"], 1)
                        if A:
                            hold(dve, go, (s["mask_ok"], 2 * u + 2))
                        for step in range(NT + 1):
                            if step < NT:
                                b = step % 2
                                k0, nt, pieces, _v = plan[step]
                                i = pc0[step]
                                if step >= 2:
                                    hold(dve, go, (s["val_tr"], u * NVC + vc0[step - 1]))
                                for c in range(2):
                                    for j, (kt, n) in enumerate(pieces):
                                        hold(dve, go, (s["score_mm"], u * NPC + i + 1))
                                        if A:
                                            o = (kt - (step - 4)) * P
                                            add = bias[:, c, o:o + n * P]
                                        elif kt + n == step + 1:
                                            add = mask[:, BAND - n * P:BAND]
                                        else:
                                            add = mask[:, 0:n * P]
                                        cs = (kt - k0) * P
                                        dve.tensor_tensor_reduce(
                                            scores(b, c)[:, cs:cs + n * P], sbank[i % 4][:, 0:n * P], add,
                                            SCALE, NEG * 8, ALU.add, ALU.max,
                                            pm[:, b, c, j:j + 1]).then_inc(s["score_ev"], 1)
                                        i += 1
                                    dve.wait_ge(s["score_ev"], u * NPC + i)
                                    ins = dve.tensor_reduce(nm[:, b, c:c + 1], pm[:, b, c, 0:len(pieces)], AX,
                                                            ALU.max, negate=True)
                                    if not A and c == 0:
                                        ch.link(ins)
                                        ins = dve.tensor_scalar(nm[:, b, 0:1], nm[:, b, 0:1], -SHIFT, None, ALU.add)
                                    ins.then_inc(s["max_ok"], 1)
                            if step >= 1:
                                t = step - 1
                                for i, h, kt, n, first, last in val_pieces(t):
                                    if i % 2:
                                        evacuate(dve, s["ev_dve"], u, i, n)
                                output(dve, u, t, ch)
                            if step < NT:
                                b = step % 2
                                dve.wait_ge(s["exp_ok"], u * 2 * NT + 2 * step + 2)
                                m = ch.add(dve.reciprocal(r[:, b, :], l[:, b, :]))
                                hold(dve, go, (s["dch"], m))
                                if not A:
                                    dve.tensor_scalar(r[:, b, 1:2], r[:, b, 1:2], lams[:, 2:3], l[:, b, 0:1],
                                                      ALU.mult, ALU.mult).then_inc(s["ratio_ok"], 1)
                                    dve.wait_ge(s["ratio_ok"], u * NT + step + 1)
                                    for kt, n in plan[step][3]:
                                        cols = slice(kt * P, (kt + n) * P)
                                        dve.scalar_tensor_tensor(S0[:, b, cols], S1[:, cols], r[:, b, 1:2],
                                                                 S0[:, b, cols], ALU.mult,
                                                                 ALU.add).then_inc(s["comb_ok"], 1)
                        assert ch.n == PER, (group, ch.n)



def pipelined(eng, step):
    for t in (-1, 0, 1, 2):
        step(t, t % 2, True, t >= 0, t >= 1, t >= 2)
    with eng.Fori(2, NT // 2) as i:
        step(2 * i - 1, 1, True, True, True, True)
        step(2 * i, 0, True, True, True, True)
    step(NT - 1, 1, False, True, True, True)
    step(NT, 0, False, False, True, True)
    step(NT + 1, 1, False, False, False, True)


def half(t):
    return t // 2


def wait(eng, sem, value):
    if not (isinstance(value, int) and value <= 0):
        eng.wait_ge(sem, value)


def stage3(nc, io, sb, sem, bank, ident, mod_d, o_d, acc_d, h2_d, list_d, table):
    with ExitStack() as ctx:
        wout = sb(ctx, "wout", [P, KT, D])
        gtm = sb(ctx, "gtm", [P, D])
        g2 = sb(ctx, "g2", [P, D])
        g2s = sb(ctx, "g2s", [P, D])
        sh2 = sb(ctx, "sh2", [P, D])
        wr = sb(ctx, "wr", [P, KT, NE])
        br = sb(ctx, "br", [P, NE])
        ot = sb(ctx, "ot", [P, 2, D])
        xt = sb(ctx, "xt3", [P, 2, D])
        oT = sb(ctx, "oT", [P, 2, KT, P])
        h2 = sb(ctx, "h2", [P, 2, D])
        h2T = sb(ctx, "h2T", [P, 2, KT, P])
        sq = sb(ctx, "sq3", [P, D])
        tmp = sb(ctx, "tmp3", [P, 2, 512])
        st = sb(ctx, "st3", [P, 4])
        hs = sb(ctx, "hs", [P, 5, B_HEADS])
        osq = sb(ctx, "osq3", [P, 2, B_HEADS, P])
        gsub = sb(ctx, "gsub", [P, P])
        tri = sb(ctx, "tri", [P, P])
        ones = sb(ctx, "ones", [P, P])
        iota = sb(ctx, "iota_e", [P, NE])
        eoff = sb(ctx, "eoff", [P, NE])
        tokc = sb(ctx, "tokc", [P, 1])
        lg = sb(ctx, "lg", [P, 2, NE])
        v8 = sb(ctx, "v8", [P, 2, 8])
        i8 = sb(ctx, "i8", [P, 2, 8], U32)
        i4 = sb(ctx, "i4", [P, 2, TOPK])
        nv = sb(ctx, "nv", [P, 2])
        ex = sb(ctx, "ex", [P, 2, TOPK])
        es = sb(ctx, "es", [P, 2])
        oh = sb(ctx, "oh", [P, 2, TOPK, NE])
        M = sb(ctx, "M", [P, 2, NE])
        macc = sb(ctx, "macc", [P, NE])
        base = sb(ctx, "base", [P, 2, NE])
        ohs = sb(ctx, "ohs", [P, TOPK, NE])
        slotf = sb(ctx, "slotf", [P, 2, TOPK])
        slot = sb(ctx, "slot", [P, 2, TOPK], I32)
        pay = sb(ctx, "pay", [P, 2, TOPK, 2])
        padl = sb(ctx, "padl", [P, PADS, 2])
        cnt = sb(ctx, "cnt", [P, 4, NE])

        (go, cin, win, oT_mm, oT_ev, mix_mm, x1_ok, sq_ok, h2_ok, hT_mm, hT_ev, lg_mm, lg_ok,
         ex_ok, nv_ok, oh_ok, rk_mm, macc_ok, slot_ok, pads, pch, pref, ini, chf, chm,
         chb, che, cmm, tab_ok, on_ok, ms_ok, rt_ok, oms_ok, ort_ok, che1) = (sem(f"s3_{n}") for n in (
            "go", "constants_in", "weights_in", "oT_product", "oT_copied", "mix_product",
            "x1_ready", "squares_summed", "h2_ready", "h2T_product", "h2T_copied", "logits_product",
            "logits_copied", "exponentials", "max_negated", "onehots_ready", "ranks_product", "counts_added",
            "slots_ready", "pads_ready", "pool_chain", "prefilled",
            "vector_constants", "front_chain", "middle_chain", "back_chain", "end_chain", "counts_product",
            "table_ready", "heads_normalised", "mean_square", "root", "heads_mean_square", "heads_root",
            "early_chain"))
        o_in, x_in, acc_out, h2_out, scat = (
            [sem(f"s3_{n}{i}") for i in range(2)] for n in ("o_in", "x_in", "acc_stored", "h2_stored", "scattered"))
        NEARLY, NF, NM, NB = 7, 4, 5, 6

        with nc.Block() as block:
            @block.sync
            def _(sp):
                sp.dma_start(wout[:, :, :], io["w_out"].rearrange("(k p) n -> p k n", p=P)).then_inc(win, 16)
                for dst, src in ((gtm, mod_d[:, 2 * D:3 * D]), (sh2, mod_d[:, 3 * D:4 * D]),
                                 (g2s, mod_d[:, 4 * D:5 * D]), (g2, io["g_ffn_norm"])):
                    sp.dma_start(dst[:, :], src.broadcast_to([P, D])).then_inc(cin, 16)
                sp.dma_start(gsub[:, :], io["g_subln"].broadcast_to([P, P])).then_inc(cin, 16)
                sp.dma_start(br[:, :], io["b_router"].broadcast_to([P, NE])).then_inc(cin, 16)
                sp.dma_start(iota[:, :], io["iota_e"].broadcast_to([P, NE])).then_inc(cin, 16)
                sp.dma_start(eoff[:, :], io["expert_offset"].broadcast_to([P, NE])).then_inc(cin, 16)
                sp.dma_start(tri[:, :], io["tri"]).then_inc(cin, 16)
                sp.dma_start(tokc[:, :], io["partition_index"]).then_inc(cin, 16)
                sp.dma_start(wr[:, :, :], io["w_router"].rearrange("(k p) n -> p k n", p=P)).then_inc(cin, 16)

                def step(t, b, early, front, middle, back):
                    if early:
                        wait(sp, oT_mm, 2 * t)
                        sp.dma_start(ot[:, 1 - b, :], o_d[bass.ds((t + 1) * P, P), :]).then_inc(o_in[1 - b], 16)
                        wait(sp, acc_out[1 - b], 16 * half(t + 1 - (1 - b)))
                        wait(sp, h2_ok, t)
                        sp.dma_start(xt[:, 1 - b, :], io["x"][bass.ds((t + 1) * P, P), :]).then_inc(x_in[1 - b], 16)
                pipelined(sp, step)

            @block.tensor
            def _(pe):
                pe.wait_ge(cin, 176)
                pe.wait_ge(ini, 3)

                def step(t, b, early, front, middle, back):
                    if front:
                        pe.wait_ge(o_in[b], 16 * half(t - b) + 16)
                        pe.wait_ge(on_ok, B_HEADS * (t + 1))
                        for h in range(2):
                            wait(pe, oT_ev, 2 * t - 1 + h)
                            for j in range(4):
                                k = 4 * h + j
                                mm = pe.transpose(bank[h][:, j * P:(j + 1) * P], ot[:, b, k * P:(k + 1) * P],
                                                  ident[:, :])
                            mm.then_inc(oT_mm, 1)
                        pe.wait_ge(oT_ev, 2 * t + 2)
                        pe.wait_ge(win, 16)
                        for h in range(2):
                            wait(pe, x1_ok, 2 * t - 1 + h)
                            for k in range(KT):
                                mm = pe.matmul(bank[2 + h][:, :], oT[:, b, k, :], wout[:, k, h * 512:(h + 1) * 512],
                                               start=(k == 0), stop=(k == KT - 1))
                            mm.then_inc(mix_mm, 1)
                    if middle:
                        c, tm = 1 - b, t - 1
                        pe.wait_ge(h2_ok, tm + 1)
                        for h in range(2):
                            wait(pe, hT_ev, 2 * tm - 1 + h)
                            for j in range(4):
                                k = 4 * h + j
                                mm = pe.transpose(bank[4 + h][:, j * P:(j + 1) * P], h2[:, c, k * P:(k + 1) * P],
                                                  ident[:, :])
                            mm.then_inc(hT_mm, 1)
                        pe.wait_ge(hT_ev, 2 * tm + 2)
                        wait(pe, lg_ok, tm)
                        for k in range(KT):
                            mm = pe.matmul(bank[6][:, 0:NE], h2T[:, c, k, :], wr[:, k, :],
                                           start=(k == 0), stop=(k == KT - 1))
                        mm.then_inc(lg_mm, 1)
                    if back:
                        tb = t - 2
                        pe.wait_ge(oh_ok, tb + 1)
                        pe.wait_ge(macc_ok, tb + 1)
                        pe.matmul(bank[7][:, 0:NE], tri[:, :], M[:, b, :], start=True, stop=False)
                        pe.matmul(bank[7][:, 0:NE], ones[:, :], macc[:, :], start=False,
                                  stop=True).then_inc(rk_mm, 1)
                pipelined(pe, step)
                pe.wait_ge(macc_ok, NT + 1)
                pe.matmul(bank[7][:, 0:NE], ones[:, :], macc[:, :], start=True, stop=True).then_inc(cmm, 1)

            @block.scalar
            def _(act):
                def step(t, b, early, front, middle, back):
                    if front:
                        for h in range(2):
                            act.wait_ge(oT_mm, 2 * t + 1 + h)
                            wait(act, mix_mm, 2 * (t - 1))
                            act.activation(oT[:, b, 4 * h:4 * h + 4, :].rearrange("p a b -> p (a b)"),
                                           bank[h][:, :], ACT.Copy).then_inc(oT_ev, 1)
                    if early:
                        act.wait_ge(oms_ok, t + 2)
                        act.activation(hs[:, 2, :], hs[:, 1, :], ACT.Sqrt).then_inc(ort_ok, 1)
                    if front:
                        act.wait_ge(x1_ok, 2 * t + 2)
                        wait(act, h2_ok, t)
                        act.activation(sq[:, :], xt[:, b, :], ACT.Square, accum_out=st[:, 0:1]).then_inc(sq_ok, 1)
                        act.wait_ge(ms_ok, t + 1)
                        act.activation(st[:, 2:3], st[:, 1:2], ACT.Sqrt).then_inc(rt_ok, 1)
                    if middle:
                        c, tm = 1 - b, t - 1
                        for h in range(2):
                            act.wait_ge(hT_mm, 2 * tm + 1 + h)
                            wait(act, lg_mm, tm - 1)
                            act.activation(h2T[:, c, 4 * h:4 * h + 4, :].rearrange("p a b -> p (a b)"),
                                           bank[4 + h][:, :], ACT.Copy).then_inc(hT_ev, 1)
                        act.wait_ge(nv_ok, tm + 1)
                        act.activation(ex[:, c, :], v8[:, c, 0:TOPK], ACT.Exp, bias=nv[:, c:c + 1],
                                       accum_out=es[:, c:c + 1]).then_inc(ex_ok, 1)
                pipelined(act, step)

            @block.gpsimd
            def _(pool):
                ch = Chain(pool, pch)
                padi = padl[:, :, :].bitcast(I32)
                ch.link(pool.memset(padl[:, :, :], 0.0))
                pool.iota(padi[:, :, 0], [[1, PADS]], base=SEQ, channel_multiplier=0).then_inc(pads, 1)
                ch.link(pool.memset(sq[:, :], 0.0))
                for dst in (acc_d, h2_d):
                    for i in range(PADS // P):
                        pool.dma_start(dst[SEQ + i * P:SEQ + (i + 1) * P, :], sq[:, :]).then_inc(pref, 16)
                pool.wait_ge(pads, 1)
                pool.dma_start(list_d.rearrange("(p a) b -> p a b", p=P), padl[:, :, :]).then_inc(pref, 16)
                pool.wait_ge(pref, 16 * (1 + 2 * PADS // P))
                pool.sem_inc(go, 1)

                def step(t, b, early, front, middle, back):
                    if front:
                        hold(pool, go, (x1_ok, 2 * t + 2))
                        pool.dma_start(acc_d[bass.ds(t * P, P), :], xt[:, b, :]).then_inc(acc_out[b], 16)
                        hold(pool, go, (h2_ok, t + 1))
                        pool.dma_start(h2_d[bass.ds(t * P, P), :], h2[:, b, :]).then_inc(h2_out[b], 16)
                    if back:
                        tb = t - 2
                        hold(pool, go, (slot_ok, tb + 1))
                        for k in range(TOPK):
                            pool.indirect_dma_start(
                                list_d, bass.IndirectOffsetOnAxis(ap=slot[:, b, k:k + 1], axis=0),
                                pay[:, b, k, :], None).then_inc(scat[b], 16)
                pipelined(pool, step)
                for b in range(2):
                    pool.wait_ge(acc_out[b], 8 * NT)
                    pool.wait_ge(h2_out[b], 8 * NT)
                    pool.wait_ge(scat[b], 8 * NT * TOPK)

            @block.vector
            def _(dve):
                dve.wait_ge(cin, 176)
                dve.memset(ones[:, :], 1.0).then_inc(ini, 1)
                dve.memset(macc[:, :], 0.0).then_inc(ini, 1)
                dve.sem_inc(macc_ok, 1)
                dve.tensor_scalar(g2s[:, :], g2s[:, :], 1.0, None, ALU.add).then_inc(ini, 1)
                dve.wait_ge(ini, 3)
                dve.tensor_tensor(g2[:, :], g2[:, :], g2s[:, :], ALU.mult).then_inc(ini, 1)
                dve.tensor_scalar(gsub[:, :], gsub[:, :], 1.0 - LAM0, None, ALU.mult).then_inc(ini, 1)
                dve.wait_ge(ini, 5)
                dve.wait_ge(pref, 16 * (1 + 2 * PADS // P))

                def step(t, b, early, front, middle, back):
                    if early:
                        ch = Chain(dve, che1, (t + 1) * NEARLY)
                        c = 1 - b
                        dve.wait_ge(o_in[c], 16 * half(t + 1 - c) + 16)
                        heads = ot[:, c, AW:D].rearrange("p (h d) -> p h d", h=B_HEADS)
                        ch.link(dve.tensor_scalar(osq[:, 0, :, :], heads, -2.0 ** 100, 2.0 ** 100, ALU.max, ALU.min))
                        ch.link(dve.scalar_tensor_tensor(osq[:, 1, :, :], osq[:, 0, :, :], 2.0 ** -80,
                                                         osq[:, 0, :, :], ALU.mult, ALU.mult))
                        ch.link(dve.tensor_reduce(hs[:, 0, :], osq[:, 1, :, :], AX, ALU.add))
                        ch.link(dve.tensor_scalar(hs[:, 3, :], hs[:, 0, :], 2.0 ** 48, 2.0 ** -40, ALU.is_le, ALU.mult))
                        ch.link(dve.tensor_scalar(hs[:, 1, :], hs[:, 0, :], 1.0 / P, EPS * 2.0 ** -80, ALU.mult, ALU.add))
                        dve.tensor_scalar(hs[:, 1, :], hs[:, 1, :], 2.0 ** 100, None, ALU.min).then_inc(oms_ok, 1)
                        dve.wait_ge(ort_ok, t + 2)
                        ch.link(dve.reciprocal(hs[:, 4, :], hs[:, 2, :]))
                        ch.link(dve.tensor_tensor(hs[:, 4, :], hs[:, 4, :], hs[:, 3, :], ALU.mult))
                        for h in range(B_HEADS):
                            dve.scalar_tensor_tensor(heads[:, h, :], heads[:, h, :], hs[:, 4, h:h + 1], gsub[:, :],
                                                     ALU.mult, ALU.mult).then_inc(on_ok, 1)
                        assert ch.n == NEARLY
                    if front:
                        ch = Chain(dve, chf, t * NF)
                        dve.wait_ge(x_in[b], 16 * half(t - b) + 16)
                        for h in range(2):
                            cs = slice(h * 512, (h + 1) * 512)
                            dve.wait_ge(mix_mm, 2 * t + 1 + h)
                            ch.link(dve.tensor_tensor(tmp[:, h, :], bank[2 + h][:, :], gtm[:, cs], ALU.mult))
                            dve.tensor_tensor(xt[:, b, cs], xt[:, b, cs], tmp[:, h, :], ALU.add).then_inc(x1_ok, 1)
                        dve.wait_ge(sq_ok, t + 1)
                        dve.tensor_scalar(st[:, 1:2], st[:, 0:1], 1.0 / D, EPS, ALU.mult, ALU.add).then_inc(ms_ok, 1)
                        dve.wait_ge(rt_ok, t + 1)
                        ch.link(dve.reciprocal(st[:, 3:4], st[:, 2:3]))
                        wait(dve, h2_out[b], 16 * half(t - b))
                        wait(dve, hT_mm, 2 * (t - 1))
                        ch.link(dve.scalar_tensor_tensor(h2[:, b, :], xt[:, b, :], st[:, 3:4], g2[:, :],
                                                         ALU.mult, ALU.mult))
                        dve.tensor_tensor(h2[:, b, :], h2[:, b, :], sh2[:, :], ALU.add).then_inc(h2_ok, 1)
                        assert ch.n == NF
                    if middle:
                        c, tm = 1 - b, t - 1
                        ch = Chain(dve, chm, tm * NM)
                        dve.wait_ge(lg_mm, tm + 1)
                        dve.tensor_tensor(lg[:, c, :], bank[6][:, 0:NE], br[:, :], ALU.add).then_inc(lg_ok, 1)
                        hold(dve, ini, (lg_ok, tm + 1))
                        m = ch.add(dve.max(v8[:, c, :], lg[:, c, :]))
                        hold(dve, ini, (chm, m))
                        ch.link(dve.max_index(i8[:, c, :], v8[:, c, :], lg[:, c, :]))
                        dve.tensor_scalar(nv[:, c:c + 1], v8[:, c, 0:1], -1.0, None, ALU.mult).then_inc(nv_ok, 1)
                        ch.link(dve.tensor_copy(i4[:, c, :], i8[:, c, 0:TOPK]))
                        for k in range(TOPK):
                            ins = dve.tensor_scalar(oh[:, c, k, :], iota[:, :], i4[:, c, k:k + 1], None,
                                                    ALU.is_equal)
                        ch.link(ins)
                        dve.tensor_reduce(M[:, c, :], oh[:, c, :, :].rearrange("p k e -> p e k"), AX,
                                          ALU.add).then_inc(oh_ok, 1)
                        dve.wait_ge(ex_ok, tm + 1)
                        ch.link(dve.reciprocal(es[:, c:c + 1], es[:, c:c + 1]))
                        assert ch.n == NM
                    if back:
                        tb = t - 2
                        ch = Chain(dve, chb, tb * NB)
                        wait(dve, scat[b], 16 * TOPK * half(tb - b))
                        dve.wait_ge(rk_mm, tb + 1)
                        dve.tensor_scalar(pay[:, b, :, 1], ex[:, b, :], es[:, b:b + 1], None, ALU.mult)
                        dve.tensor_copy(pay[:, b, :, 0].bitcast(I32), tokc[:, 0:1].broadcast_to([P, TOPK]))
                        ch.link(dve.tensor_tensor(base[:, b, :], bank[7][:, 0:NE], eoff[:, :], ALU.add))
                        ch.link(dve.tensor_scalar(tokc[:, :], tokc[:, :], float(P), None, ALU.add))
                        dve.tensor_tensor(macc[:, :], macc[:, :], M[:, b, :], ALU.add).then_inc(macc_ok, 1)
                        for k in range(TOPK):
                            ch.link(dve.tensor_tensor_reduce(ohs[:, k, :], oh[:, b, k, :], base[:, b, :], 1.0, 0.0,
                                                             ALU.mult, ALU.add, slotf[:, b, k:k + 1]))
                        dve.tensor_copy(slot[:, b, :], slotf[:, b, :]).then_inc(slot_ok, 1)
                        assert ch.n == NB
                pipelined(dve, step)
                ch = Chain(dve, che)
                dve.wait_ge(cmm, 1)
                ch.link(dve.tensor_copy(cnt[:, 0, :], bank[7][:, 0:NE]))
                ch.link(dve.memset(cnt[:, 1, :], 1.0))
                for j in range(1, CAP // TOK):
                    ch.link(dve.scalar_tensor_tensor(cnt[:, 1, :], cnt[:, 0, :], float(j * TOK), cnt[:, 1, :],
                                                     ALU.is_gt, ALU.add))
                ch.link(dve.tensor_tensor_scan(cnt[:, 2, :], ones[:, 0:NE], cnt[:, 1, :], 0.0, ALU.mult, ALU.add))
                ch.link(dve.tensor_tensor(cnt[:, 3, :], cnt[:, 2, :], cnt[:, 1, :], ALU.subtract))
                ch.link(dve.tensor_copy(table[0:1, 0:NE], cnt[0:1, 1, :]))
                ch.link(dve.tensor_copy(table[0:1, NE:2 * NE], cnt[0:1, 3, :]))
                ch.link(dve.tensor_copy(table[0:1, 2 * NE:2 * NE + 1], cnt[0:1, 2, NE - 1:NE]))
                ch.link(dve.scalar_tensor_tensor(cnt[:, 0, :], cnt[:, 1, :], float(-TOK), cnt[:, 0, :],
                                                 ALU.mult, ALU.add))
                ch.link(dve.tensor_scalar(cnt[:, 2, :], cnt[:, 0, :], float(SMALL - TOK), None, ALU.is_le))
                ch.link(dve.tensor_tensor(cnt[:, 3, :], cnt[:, 1, :], cnt[:, 2, :], ALU.subtract))
                ch.link(dve.tensor_copy(table[0:1, 3 * NE:4 * NE], cnt[0:1, 3, :]))
                ch.link(dve.tensor_copy(table[0:1, 4 * NE:5 * NE], cnt[0:1, 2, :]))


def stage4(nc, io, sb, sem, bank, ident, mod_d, acc_d, h2_d, list_d, table):
    RAW, SPL = 3, 3
    UPT, PPT = 12, 6
    MT = D // P
    def subtiles(tok):
        return [(s, min(P, tok - s * P)) for s in range(-(-tok // P))]

    subs = subtiles(TOK)
    NS = len(subs)
    batch_after = {TOK: {(0, 1): 0, (0, 2): 1, (1, 1): 2, (2, 0): 3, (2, 1): 4, (2, 2): 5},
                   SMALL: {(0, 1): 0, (1, 0): 1, (1, 1): 2, (2, 0): 3, (2, 1): 4, (3, 0): 5}}
    NX = 2 * NS
    with ExitStack() as ctx:
        raw = sb(ctx, "raw", [P, RAW, 2, KT, 256])
        hi = [sb(ctx, f"w_hi{i}", [P, 2048], F32R) for i in range(SPL)]
        lo = [sb(ctx, f"w_lo{i}", [P, 2048], F32R) for i in range(SPL)]
        xg = sb(ctx, "xg", [P, NS, D])
        x_hi = sb(ctx, "x_hi", [P, KT, TOK], F32R)
        x_lo = sb(ctx, "x_lo", [P, KT, TOK], F32R)
        a_hi = sb(ctx, "a_hi", [P, MT, TOK], F32R)
        a_lo = sb(ctx, "a_lo", [P, MT, TOK], F32R)
        a = sb(ctx, "a", [P, 2, TOK])
        gate = sb(ctx, "gate", [P, TOK])
        sig = sb(ctx, "sig", [P, TOK])
        up = sb(ctx, "up", [P, TOK])
        bgu = sb(ctx, "bgu", [P, NE * 2 * MT])
        bcur = sb(ctx, "bcur", [P, 2 * MT])
        bd = sb(ctx, "bd", [P, D])
        gtf = sb(ctx, "gtf", [P, D])
        y = sb(ctx, "y", [P, NS, D])
        idn = sb(ctx, "idn", [P, NS, 2])
        idc = sb(ctx, "idc", [P, NS, 2])
        pidx = sb(ctx, "pidx", [P, 1])

        (go, cin, bd_in, gu_mm, g_ev, tx_mm, xhi_ok, xlo_ok, a_ok, ahi_ok, alo_ok, dn_mm, yb_ok, y_ok,
         hi_ok, lo_ok, li, xg_in, sc, idc_ok, sig_ok, gch, bc_ok, pch,
         cleared) = (sem(f"s4_{n}") for n in (
            "go", "constants_in", "bias_down_in", "gate_up_product", "gate_up_read", "x_transposed",
            "x_high", "x_low", "act_ready", "act_high", "act_low", "down_product", "down_read", "y_ready",
            "weights_high", "weights_low", "list_in", "rows_gathered", "scattered", "ids_current",
            "sigmoid_ready", "vector_chain", "bias_current", "pool_chain", "rows_cleared"))
        raw_in = [sem(f"s4_raw_in{i}") for i in range(RAW)]
        NG = 2 * MT
        LO0 = 2 * RAW

        def expert_tiles(eng, e):
            n = eng.value_load(table[0:1, bass.ds(e, 1)], min_val=1, max_val=CAP // TOK)
            b = eng.value_load(table[0:1, bass.ds(e + NE, 1)], min_val=0, max_val=TOPK * SEQ // TOK + NE)
            return n, b

        def over_sizes(eng, tile):
            with eng.Fori(0, NE) as e:
                full = eng.value_load(table[0:1, bass.ds(e + 3 * NE, 1)], min_val=0, max_val=CAP // TOK)
                small = eng.value_load(table[0:1, bass.ds(e + 4 * NE, 1)], min_val=0, max_val=1)
                _, before = expert_tiles(eng, e)
                with eng.If(full > 0):
                    with eng.Fori(0, full) as r:
                        tile(e, before + r, TOK)
                with eng.If(small > 0):
                    tile(e, before + full, SMALL)

        def through(s, tok):
            return NS if s == len(subtiles(tok)) - 1 else s + 1

        def step_of(s, tok):
            return through(s, tok) - s

        def over_tiles(eng, tile):
            with eng.Fori(0, NE) as e:
                n, before = expert_tiles(eng, e)
                with eng.Fori(0, n) as r:
                    tile(e, r, before + r)

        def total_tiles(eng):
            return eng.value_load(table[0:1, 2 * NE:2 * NE + 1], min_val=NE, max_val=TOPK * SEQ // TOK + NE)

        def split_views(u):
            slot, half_ = (u // 2) % RAW, u % 2
            h, l = hi[u % SPL], lo[u % SPL]
            if u < MT:
                src = raw[:, slot, :, :, half_ * P:(half_ + 1) * P].rearrange("p o k n -> p (o k) n")
                return src, h[:, :].rearrange("p (a n) -> p a n", n=P), l[:, :].rearrange("p (a n) -> p a n", n=P)
            src = raw[:, slot, half_, :, :].rearrange("p k n -> p (k n)")
            return src, h[:, :], l[:, :]

        def raw_arrived(eng, u, g):
            p = u // 2
            eng.wait_ge(raw_in[p % RAW], 32 * (2 * g + p // RAW) + 32)

        with nc.Block() as block:
            @block.sync
            def _(sp):
                def load_pair(e, p, g):
                    sp.wait_ge(lo_ok, UPT * g + 2 * p + 2)
                    slot = p % RAW
                    if p < 4:
                        for o in range(2):
                            c0 = o * D + p * 256
                            sp.dma_start(raw[:, slot, o, :, :], io["w_gate_up"][bass.ds(e, 1), :, c0:c0 + 256]
                                         .rearrange("o (k p) n -> p (o k) n", p=P)).then_inc(raw_in[slot], 16)
                    else:
                        for kh in range(2):
                            sp.dma_start(raw[:, slot, kh, :, :].rearrange("p k n -> p (k n)")
                                         .rearrange("p (k n) -> p k n", n=512),
                                         io["w_down"][bass.ds(e, 1), kh * 512:(kh + 1) * 512,
                                                      (p - 4) * 512:(p - 3) * 512]
                                         .rearrange("o (k p) n -> p (o k) n", p=P)).then_inc(raw_in[slot], 16)

                def tile(e, r, g):
                    for p in range(PPT):
                        load_pair(e, p, g)
                        if p == 4:
                            sp.wait_ge(y_ok, NX * g)
                            sp.dma_start(bd[:, :], io["b_down"][bass.ds(e, 1), :].broadcast_to([P, D])).then_inc(bd_in, 16)

                sp.dma_start(bgu[:, :], io["b_gate_up_col"]).then_inc(cin, 16)
                sp.dma_start(gtf[:, :], mod_d[:, 5 * D:6 * D].broadcast_to([P, D])).then_inc(cin, 16)
                sp.dma_start(pidx[:, :], io["partition_index"]).then_inc(cin, 16)
                over_tiles(sp, tile)
                total = total_tiles(sp)
                for p in range(2):
                    load_pair(NE - 1, p, total)

            @block.tensor
            def _(pe):
                def transpose_x(g, j):
                    s, h = j // 2, j % 2
                    if not (isinstance(g, int) and j == 0):
                        pe.wait_ge(xlo_ok, NX * g + j)
                    for i in range(4):
                        k = 4 * h + i
                        mm = pe.transpose(bank[7][:, i * P:(i + 1) * P], xg[:, s, k * P:(k + 1) * P], ident[:, :])
                    mm.then_inc(tx_mm, 1)

                def tile(e, g, tok):
                    pe.wait_ge(xlo_ok, NX * g + NX)
                    for m in range(MT):
                        pe.wait_ge(lo_ok, UPT * g + m + 1 + LO0)
                        if m >= 2:
                            pe.wait_ge(g_ev, 2 * MT * g + 2 * (m - 2) + 2)
                        for o in range(2):
                            out = bank[2 * (m % 2) + o][:, 0:tok]
                            for k in range(KT):
                                at = slice((o * KT + k) * P, (o * KT + k + 1) * P)
                                pe.matmul(out, hi[m % SPL][:, at], x_hi[:, k, 0:tok], start=(k == 0), stop=False)
                                pe.matmul(out, hi[m % SPL][:, at], x_lo[:, k, 0:tok], start=False, stop=False)
                                mm = pe.matmul(out, lo[m % SPL][:, at], x_hi[:, k, 0:tok], start=False,
                                               stop=(k == KT - 1))
                            mm.then_inc(gu_mm, 1)
                    pe.wait_ge(xg_in, 16 * NS * g + 32 * NS)
                    for c in range(2):
                        for kh in range(2):
                            d = 2 * c + kh
                            u = MT + d
                            pe.wait_ge(lo_ok, UPT * g + u + 1 + LO0)
                            if c == 0:
                                pe.wait_ge(alo_ok, MT * g + 4 * kh + 4)
                            for s, rows in subtiles(tok):
                                if d == 2:
                                    pe.wait_ge(yb_ok, NX * g + through(s, tok))
                                tk = slice(s * P, s * P + rows)
                                out = bank[4 + s][0:rows, :]
                                for i in range(4):
                                    k, at = 4 * kh + i, slice(i * 512, (i + 1) * 512)
                                    pe.matmul(out, a_hi[:, k, tk], hi[u % SPL][:, at], start=(kh == 0 and i == 0),
                                              stop=False)
                                    pe.matmul(out, a_hi[:, k, tk], lo[u % SPL][:, at], start=False, stop=False)
                                    mm = pe.matmul(out, a_lo[:, k, tk], hi[u % SPL][:, at], start=False,
                                                   stop=(kh == 1 and i == 3))
                                mm.then_inc(dn_mm, step_of(s, tok))
                                if (d, s) in batch_after[tok]:
                                    transpose_x(g + 1, batch_after[tok][d, s])

                pe.wait_ge(xg_in, 16 * NS)
                for j in range(NX):
                    transpose_x(0, j)
                over_sizes(pe, tile)

            @block.scalar
            def _(act):
                def split_hi(u, g):
                    raw_arrived(act, u, g)
                    src, h, _ = split_views(u)
                    act.activation(h, src, ACT.Copy).then_inc(hi_ok, 1)

                def split_next(u, g):
                    if u < MT:
                        act.wait_ge(gu_mm, 2 * MT * g + 2 * u + 2)
                    else:
                        act.wait_ge(dn_mm, 4 * NS * g + NS * (u - MT + 1))
                    split_hi((u + SPL) % UPT, g + (u + SPL) // UPT)

                def x_high(g, j):
                    (s, rows), h = subs[j // 2], j % 2
                    act.wait_ge(tx_mm, NX * g + j + 1)
                    act.activation(x_hi[:, 4 * h:4 * h + 4, s * P:s * P + rows],
                                   bank[7][:, :].rearrange("p (k n) -> p k n", n=P)[:, :, 0:rows],
                                   ACT.Copy).then_inc(xhi_ok, 1)

                def tile(e, g, tok):
                    for m in range(MT):
                        act.wait_ge(g_ev, 2 * MT * g + 2 * m + 1)
                        act.activation(sig[:, 0:tok], gate[:, 0:tok], ACT.Sigmoid, scale=ALPHA).then_inc(sig_ok, 1)
                        split_next(m, g)
                        act.wait_ge(a_ok, MT * g + m + 1)
                        act.activation(a_hi[:, m, 0:tok], a[:, m % 2, 0:tok], ACT.Copy).then_inc(ahi_ok, 1)
                    for d in range(4):
                        for s in range(NS):
                            if (d, s) in batch_after[tok]:
                                x_high(g + 1, batch_after[tok][d, s])
                        split_next(MT + d, g)

                for u in range(SPL):
                    split_hi(u, 0)
                for j in range(NX):
                    x_high(0, j)
                over_sizes(act, tile)

            @block.vector
            def _(dve):
                def split_lo(u, g):
                    dve.wait_ge(hi_ok, UPT * g + u + 1)
                    src, h, l = split_views(u)
                    dve.tensor_tensor(l, src, h, ALU.subtract).then_inc(lo_ok, 1)

                def split_next(u, g):
                    split_lo((u + SPL) % UPT, g + (u + SPL) // UPT)

                def x_low(g, j):
                    (s, rows), h = subs[j // 2], j % 2
                    dve.wait_ge(xhi_ok, NX * g + j + 1)
                    dst = (slice(None), slice(4 * h, 4 * h + 4), slice(s * P, s * P + rows))
                    dve.tensor_tensor(x_lo[dst], bank[7][:, :].rearrange("p (k n) -> p k n", n=P)[:, :, 0:rows],
                                      x_hi[dst], ALU.subtract).then_inc(xlo_ok, 1)

                def act_low(g, m, tok):
                    dve.wait_ge(ahi_ok, MT * g + m + 1)
                    dve.tensor_tensor(a_lo[:, m, 0:tok], a[:, m % 2, 0:tok], a_hi[:, m, 0:tok],
                                      ALU.subtract).then_inc(alo_ok, 1)

                def result(g, c, s, rows, tok):
                    cs = slice(c * 512, (c + 1) * 512)
                    n = through(s, tok)
                    dve.wait_ge(dn_mm, 4 * NS * g + 2 * NS * c + NS + n)
                    dve.tensor_tensor(y[0:rows, s, cs], bank[4 + s][0:rows, :], bd[0:rows, cs],
                                      ALU.add).then_inc(yb_ok, step_of(s, tok))
                    dve.wait_ge(yb_ok, NX * g + NS * c + n)
                    dve.scalar_tensor_tensor(y[0:rows, s, cs], y[0:rows, s, cs], idc[0:rows, s, 1:2],
                                             gtf[0:rows, cs], ALU.mult, ALU.mult).then_inc(y_ok, step_of(s, tok))

                def tile(e, g, tok):
                    ch = Chain(dve, gch, g * NG)
                    dve.tensor_copy(bcur[:, :], bgu[:, bass.ds(e * 2 * MT, 2 * MT)]).then_inc(bc_ok, 1)
                    dve.wait_ge(bc_ok, g + 1)
                    for m in range(MT):
                        dve.wait_ge(gu_mm, 2 * MT * g + 2 * m + 1)
                        dve.tensor_scalar(gate[:, 0:tok], bank[2 * (m % 2)][:, 0:tok], bcur[:, m:m + 1], LIMIT, ALU.add,
                                          ALU.min).then_inc(g_ev, 1)
                        dve.wait_ge(gu_mm, 2 * MT * g + 2 * m + 2)
                        dve.tensor_scalar(up[:, 0:tok], bank[2 * (m % 2) + 1][:, 0:tok], bcur[:, MT + m:MT + m + 1], -LIMIT,
                                          ALU.add, ALU.max).then_inc(g_ev, 1)
                        dve.wait_ge(g_ev, 2 * MT * g + 2 * m + 2)
                        ch.link(dve.tensor_scalar(up[:, 0:tok], up[:, 0:tok], LIMIT, 1.0, ALU.min, ALU.add))
                        if m:
                            act_low(g, m - 1, tok)
                        split_next(m, g)
                        dve.wait_ge(sig_ok, MT * g + m + 1)
                        ch.link(dve.tensor_tensor(gate[:, 0:tok], gate[:, 0:tok], sig[:, 0:tok], ALU.mult))
                        dve.tensor_tensor(a[:, m % 2, 0:tok], up[:, 0:tok], gate[:, 0:tok], ALU.mult).then_inc(a_ok, 1)
                        dve.wait_ge(a_ok, MT * g + m + 1)
                    act_low(g, MT - 1, tok)
                    dve.wait_ge(bd_in, 16 * g + 16)
                    dve.wait_ge(idc_ok, NS * g + NS)
                    dve.wait_ge(sc, 16 * NS * g + 16 * NS)
                    for d in range(4):
                        for s, rows in subtiles(tok):
                            if d % 2 == 1:
                                result(g, d // 2, s, rows, tok)
                            if (d, s) in batch_after[tok]:
                                x_low(g + 1, batch_after[tok][d, s])
                        split_next(MT + d, g)
                    assert ch.n == NG

                dve.sem_inc(lo_ok, LO0)
                dve.wait_ge(cin, 48)
                dve.memset(xg[:, :, :], 0.0).then_inc(cleared, 1)
                dve.wait_ge(cleared, 1)
                dve.memset(y[:, :, :], 0.0).then_inc(go, 1)
                for u in range(SPL):
                    split_lo(u, 0)
                for j in range(NX):
                    x_low(0, j)
                over_sizes(dve, tile)

            @block.gpsimd
            def _(pool):
                pool.wait_ge(cin, 48)
                pool.memset(idc[:, :, :], 0.0).then_inc(pch, 1)
                pool.wait_ge(pch, 1)
                for s in range(NS):
                    pool.tensor_scalar(idc[:, s, 0:1].bitcast(I32), pidx[:, 0:1], float(SEQ + s * P), None,
                                       ALU.add).then_inc(pch, 1)
                hold(pool, go, (pch, 1 + NS))

                def scatter():
                    for s, rows in subs:
                        pool.indirect_dma_start(
                            acc_d, bass.IndirectOffsetOnAxis(ap=idc[0:rows, s, 0:1].bitcast(I32), axis=0),
                            y[0:rows, s, :], None, compute_op=ALU.add).then_inc(sc, 16)

                def gather():
                    for s, rows in subs:
                        pool.indirect_dma_start(xg[0:rows, s, :], None, h2_d, bass.IndirectOffsetOnAxis(
                            ap=idn[0:rows, s, 0:1].bitcast(I32), axis=0)).then_inc(xg_in, 16)

                def tile(e, r, g):
                    for s, rows in subs:
                        pool.dma_start(idn[0:rows, s, :],
                                       list_d[bass.ds(e * CAP + r * TOK + s * P, rows), :]).then_inc(li, 16)
                    hold(pool, go, (li, 16 * NS * g + 16 * NS), (tx_mm, NX * g))
                    gather()
                    hold(pool, go, (y_ok, NX * g))
                    scatter()
                    hold(pool, go, (sc, 16 * NS * g + 16 * NS), (xg_in, 16 * NS * g + 16 * NS))
                    for s, rows in subs:
                        pool.tensor_copy(idc[0:rows, s, :], idn[0:rows, s, :]).then_inc(idc_ok, 1)
                    hold(pool, go, (idc_ok, NS * g + NS))

                over_tiles(pool, tile)
                total = total_tiles(pool)
                hold(pool, go, (tx_mm, NX * total))
                gather()
                hold(pool, go, (y_ok, NX * total))
                scatter()
                hold(pool, go, (sc, 16 * NS * total + 16 * NS), (xg_in, 16 * NS * total + 16 * NS))
                pool.sem_inc(go, 1)


def stage5(nc, io, sb, sem, acc_d):
    R = 4
    with ExitStack() as ctx:
        xf = sb(ctx, "xf", [P, R, D])
        yf = sb(ctx, "yf", [P, R, D])
        sq = sb(ctx, "sq5", [P, D])
        st = sb(ctx, "st5", [P, R])
        rs = sb(ctx, "rs5", [P, R])
        ms = sb(ctx, "ms5", [P, R])
        rt = sb(ctx, "rt5", [P, R])
        gf = sb(ctx, "gf", [P, D])
        cin, ss_ok, f_ok, vch, ms_ok, rt_ok = (sem(f"s5_{n}") for n in (
            "gain_in", "squares_summed", "result_ready", "vector_chain", "mean_square", "root"))
        x_in, f_out = ([sem(f"s5_{n}{i}") for i in range(R)] for n in ("rows_in", "result_stored"))
        with nc.Block() as block:
            @block.sync
            def _(sp):
                sp.dma_start(gf[:, :], io["g_final"].broadcast_to([P, D])).then_inc(cin, 16)
                with sp.Fori(0, NT // R) as i:
                    for j in range(R):
                        sp.wait_ge(f_ok, R * i + j + 1)
                        sp.dma_start(xf[:, j, :], acc_d[bass.ds((i * R + j) * P, P), :]).then_inc(x_in[j], 16)

            @block.scalar
            def _(act):
                with act.Fori(0, NT // R) as i:
                    for j in range(R):
                        act.wait_ge(x_in[j], 16 * i + 16)
                        act.wait_ge(f_ok, R * i + j + 1)
                        act.activation(sq[:, :], xf[:, j, :], ACT.Square, accum_out=st[:, j:j + 1]).then_inc(ss_ok, 1)
                        act.wait_ge(ms_ok, i * R + j + 1)
                        act.activation(rt[:, j:j + 1], ms[:, j:j + 1], ACT.Sqrt).then_inc(rt_ok, 1)

            @block.vector
            def _(dve):
                dve.sem_inc(f_ok, R)
                dve.wait_ge(cin, 16)
                with dve.Fori(0, NT // R) as i:
                    ch = Chain(dve, vch, R * i)
                    for j in range(R):
                        dve.wait_ge(ss_ok, i * R + j + 1)
                        dve.tensor_scalar(ms[:, j:j + 1], st[:, j:j + 1], 1.0 / D, EPS, ALU.mult,
                                          ALU.add).then_inc(ms_ok, 1)
                        dve.wait_ge(rt_ok, i * R + j + 1)
                        ch.link(dve.reciprocal(rs[:, j:j + 1], rt[:, j:j + 1]))
                        dve.wait_ge(f_out[j], 16 * i)
                        dve.scalar_tensor_tensor(yf[:, j, :], xf[:, j, :], rs[:, j:j + 1], gf[:, :], ALU.mult,
                                                 ALU.mult).then_inc(f_ok, 1)

            @block.gpsimd
            def _(pool):
                with pool.Fori(0, NT // R) as i:
                    for j in range(R):
                        pool.wait_ge(f_ok, i * R + j + 1 + R)
                        pool.wait_ge(cin, 16)
                        pool.dma_start(io["out"][bass.ds((i * R + j) * P, P), :], yf[:, j, :]).then_inc(f_out[j], 16)
                for j in range(R):
                    pool.wait_ge(f_out[j], 16 * NT // R)


def shape_constants():
    rot = np.zeros((P, P), np.float32)
    freq = np.zeros((P, 1), np.float32)
    theta = np.float32(500000.0) ** (-np.arange(0, 2 * ROPE_HALF, 2, dtype=np.float32) / np.float32(2 * ROPE_HALF))
    for base in (0, HD):
        for f in range(ROPE_HALF):
            lo, hi = base + f, base + ROPE_HALF + f
            rot[hi, lo] = -1.0
            rot[lo, hi] = 1.0
            freq[lo, 0] = freq[hi, 0] = theta[f]
    return {
        "ident": np.eye(P, dtype=np.float32), "rot": rot, "freq": freq,
        "tri": np.triu(np.ones((P, P), np.float32), 1),
        "iota_e": np.arange(NE, dtype=np.float32)[None, :],
        "expert_offset": (np.arange(NE, dtype=np.float32) * CAP)[None, :],
        "partition_index": np.arange(P, dtype=np.float32)[:, None],
    }


def kernel(**inputs):
    import concourse.bacc as _bacc
    from concourse.bass_utils import run_bass_kernel_spmd as _run

    g = {k: np.asarray(v) for k, v in inputs.items()}
    arrays = {
        "x": g["x"][0],
        "c_col": np.ascontiguousarray(g["c"].reshape(KT, P).T),
        "g_mix_col": np.ascontiguousarray(g["g_mix_norm"].reshape(KT, P).T),
        "positions": g["positions"],
        "w_ada": g["w_ada"][0], "b_ada": g["b_ada"],
        "w_in": g["w_in"][0],
        "rel_rev": np.ascontiguousarray(g["rel_bias"][0, :, ::-1]),
        "lambdas": np.concatenate([g["lambda_q1"], g["lambda_k1"], g["lambda_q2"], g["lambda_k2"]]),
        "g_subln": g["g_subln"],
        "w_out": g["w_out"][0],
        "g_ffn_norm": g["g_ffn_norm"],
        "w_router": g["w_router"][0], "b_router": g["b_router"],
        "w_gate_up": g["w_gate_up"][0],
        "b_gate_up_col": np.ascontiguousarray(g["b_gate_up"][0].reshape(NE * 2 * D // P, P).T),
        "w_down": g["w_down"][0], "b_down": g["b_down"][0],
        "g_final": g["g_final"][None, :],
        **shape_constants(),
    }
    nc = _bacc.Bacc("TRN2", target_bir_lowering=False, num_devices=1)
    io = {n: nc.dram_tensor(f"in_{n}", a.shape, mybir.dt.from_np(a.dtype), kind="ExternalInput").ap()
          for n, a in arrays.items()}
    for n, shape in (("mod_scratch", (1, NMOD * D)), ("o_scratch", (SEQ, D)), ("acc_scratch", (ROWS, D)),
                     ("h2_scratch", (ROWS, D)), ("list_scratch", (NE * CAP, 2)), ("toe_scratch", (A_HEADS, TOE)),
                     ("bias_scratch", (A_HEADS, P, TOE))):
        io[n] = nc.dram_tensor(n, shape, F32, kind="Internal").ap()
    io["out"] = nc.dram_tensor("out_0", (SEQ, D), F32, kind="ExternalOutput").ap()
    build_program(nc, io)
    r = _run(nc, [{f"in_{n}": a for n, a in arrays.items()}], core_ids=[0])
    return r.results[0]["out_0"].reshape(1, SEQ, D)
```
